# Optimizing a Trainium2 kernel written in Bass

```python
import math
import jax, jax.numpy as jnp
from jax import lax
import numpy as np

D_MODEL = 1024
BATCH = 1
SEQ = 1024
DEPTH = 2

D_MIX = D_MODEL
HEAD_DIM = 64
D_M = D_MIX // 4
M_HEADS = D_M // HEAD_DIM
M_CHUNK = 64
D_A = D_MIX // 4
A_HEADS = D_A // HEAD_DIM
IDX_HEADS = 4
IDX_DIM = 64
TOPK_MAX = 256
Q_BLOCK = 128
D_S = D_MIX // 2
S_HEADS = D_S // HEAD_DIM
S_GROUPS = 2
S_STATE = 128
S_CONV = 4
S_CHUNK = 64
CONV_DIM = D_S + 2 * S_GROUPS * S_STATE
ROPE_THETA = 500000.0
ROPE_DIM = HEAD_DIM // 4
D_FF = -(-8 * D_MODEL // (3 * 256)) * 256
EPS = 1e-6
N_IN = (4 * D_M + 2 * M_HEADS) + (3 * D_A + IDX_HEADS * IDX_DIM + IDX_DIM + IDX_HEADS) + (D_S + CONV_DIM + S_HEADS)

kernel_name = "hymba_style_mlstm_dsa_ssd_hybrid"

def _split_points():
    sizes = (D_M, D_M, D_M, D_M, M_HEADS, M_HEADS,
             D_A, D_A, D_A, IDX_HEADS * IDX_DIM, IDX_DIM, IDX_HEADS,
             D_S, CONV_DIM, S_HEADS)
    return [int(v) for v in np.cumsum(sizes)[:-1]]

def rms_norm(x, w):
    xf = x.astype(jnp.float32)
    y = xf * lax.rsqrt(jnp.mean(xf * xf, axis=-1, keepdims=True) + EPS)
    return (y * w.astype(jnp.float32)).astype(x.dtype)

def rope_partial(x, positions):
    half = ROPE_DIM // 2
    inv_freq = jnp.power(jnp.float32(ROPE_THETA), -jnp.arange(half, dtype=jnp.float32) / half)
    ang = positions.astype(jnp.float32)[..., None] * inv_freq
    cos = jnp.cos(ang)[:, :, None, :]
    sin = jnp.sin(ang)[:, :, None, :]
    x1 = x[..., :half].astype(jnp.float32)
    x2 = x[..., half:ROPE_DIM].astype(jnp.float32)
    rot = jnp.concatenate([x1 * cos - x2 * sin, x2 * cos + x1 * sin], axis=-1).astype(x.dtype)
    return jnp.concatenate([rot, x[..., ROPE_DIM:]], axis=-1)

def mlstm_chunkwise(q, k, v, i_pre, f_pre):
    B, S, H, d = q.shape
    L = M_CHUNK
    nc = S // L
    f32 = jnp.float32

    def to_chunks(t):
        t = t.reshape(B, nc, L, H, *t.shape[3:])
        return jnp.moveaxis(t, (1, 3), (0, 2))

    qc = to_chunks(q.astype(f32) * (d ** -0.5))
    kc = to_chunks(k.astype(f32))
    vc = to_chunks(v.astype(f32))
    ic = to_chunks(i_pre.astype(f32))
    lfc = to_chunks(jax.nn.log_sigmoid(f_pre.astype(f32)))
    causal = jnp.tril(jnp.ones((L, L), dtype=bool))

    def step(carry, inp):
        C, n, m = carry
        qb, kb, vb, ib, lfb = inp
        b = jnp.cumsum(lfb, axis=-1)
        log_d = jnp.where(causal, b[..., :, None] - b[..., None, :] + ib[..., None, :], -jnp.inf)
        m_inter = b + m[..., None]
        m_t = jnp.maximum(m_inter, jnp.max(log_d, axis=-1))
        s = jnp.einsum('bhtd,bhsd->bhts', qb, kb) * jnp.exp(log_d - m_t[..., None])
        scale = jnp.exp(m_inter - m_t)
        num = (jnp.einsum('bhts,bhsd->bhtd', s, vb)
               + scale[..., None] * jnp.einsum('bhtd,bhde->bhte', qb, C))
        den = jnp.sum(s, axis=-1) + scale * jnp.einsum('bhtd,bhd->bht', qb, n)
        h = num / jnp.maximum(jnp.abs(den), jnp.exp(-m_t))[..., None]
        b_last = b[..., -1]
        log_w = b_last[..., None] - b + ib
        m_new = jnp.maximum(b_last + m, jnp.max(log_w, axis=-1))
        w = jnp.exp(log_w - m_new[..., None])
        decay = jnp.exp(b_last + m - m_new)
        C_new = decay[..., None, None] * C + jnp.einsum('bhs,bhsd,bhse->bhde', w, kb, vb)
        n_new = decay[..., None] * n + jnp.einsum('bhs,bhsd->bhd', w, kb)
        return (C_new, n_new, m_new), h

    init = (jnp.zeros((B, H, d, d), f32), jnp.zeros((B, H, d), f32), jnp.zeros((B, H), f32))
    _, hc = lax.scan(step, init, (qc, kc, vc, ic, lfc))
    return jnp.moveaxis(hc, (0, 2), (1, 3)).reshape(B, S, H, d)

def dsa_attention(q, k, v, q_idx, k_idx, w_idx):
    B, S, H, d = q.shape
    top_k = min(TOPK_MAX, S // 4)
    nb = S // Q_BLOCK
    f32 = jnp.float32
    key_pos = jnp.arange(S)
    k_idx_f = k_idx.astype(f32)

    def blocks(t):
        return jnp.moveaxis(t.reshape(B, nb, Q_BLOCK, *t.shape[2:]), 1, 0)

    def one_block(inp):
        qb, qib, wb, qpos = inp
        dots = jnp.einsum('bthd,bsd->bths', qib.astype(f32), k_idx_f) * (IDX_DIM ** -0.5)
        score = jnp.einsum('bth,bths->bts', wb.astype(f32), jax.nn.relu(dots))
        causal = key_pos[None, :] <= qpos[:, None]
        score = jnp.where(causal[None], score, -jnp.inf)
        _, sel = lax.top_k(score, top_k)
        valid = sel <= qpos[None, :, None]
        k_sel = jax.vmap(lambda kk, ii: kk[ii])(k, sel)
        v_sel = jax.vmap(lambda vv, ii: vv[ii])(v, sel)
        logits = jnp.einsum('bthd,btkhd->bthk', qb.astype(f32), k_sel.astype(f32)) * (d ** -0.5)
        logits = jnp.where(valid[:, :, None, :], logits, -jnp.inf)
        p = jax.nn.softmax(logits, axis=-1)
        return jnp.einsum('bthk,btkhd->bthd', p, v_sel.astype(f32))

    out = lax.map(one_block, (blocks(q), blocks(q_idx), blocks(w_idx),
                              jnp.arange(S).reshape(nb, Q_BLOCK)))
    return jnp.moveaxis(out, 0, 1).reshape(B, S, H, d)

def ssd_chunked(x, dt, A, Bh, Ch):
    B, S, H, P = x.shape
    N = Bh.shape[-1]
    L = S_CHUNK
    nc = S // L

    def to_chunks(t):
        return jnp.moveaxis(t.reshape(B, nc, L, *t.shape[2:]), 1, 0)

    causal = jnp.tril(jnp.ones((L, L), dtype=bool))

    def step(state, inp):
        xb, dtb, Bb, Cb = inp
        acum = jnp.cumsum(dtb * A, axis=1)
        seg = jnp.where(causal[None, :, :, None], acum[:, :, None, :] - acum[:, None, :, :], -jnp.inf)
        scores = jnp.einsum('bthn,bshn->btsh', Cb, Bb) * jnp.exp(seg)
        y_intra = jnp.einsum('btsh,bshp->bthp', scores, xb * dtb[..., None])
        y_inter = jnp.einsum('bthn,bhpn->bthp', Cb, state) * jnp.exp(acum)[..., None]
        a_last = acum[:, -1]
        w = jnp.exp(a_last[:, None, :] - acum) * dtb
        state_new = (state * jnp.exp(a_last)[..., None, None]
                     + jnp.einsum('bshn,bsh,bshp->bhpn', Bb, w, xb))
        return state_new, y_intra + y_inter

    init = jnp.zeros((B, H, P, N), jnp.float32)
    _, yc = lax.scan(step, init, (to_chunks(x), to_chunks(dt), to_chunks(Bh), to_chunks(Ch)))
    return jnp.moveaxis(yc, 0, 1).reshape(B, S, H, P)

def ssd_mixer(xbc_raw, z, dt_raw, conv_w, conv_b, dt_bias, a_log, d_skip, norm_w):
    B, S, _ = xbc_raw.shape
    f32 = jnp.float32
    xbc = lax.conv_general_dilated(
        xbc_raw, conv_w[:, None, :], window_strides=(1,), padding=[(S_CONV - 1, 0)],
        dimension_numbers=('NWC', 'WIO', 'NWC'), feature_group_count=CONV_DIM) + conv_b
    xbc = jax.nn.silu(xbc.astype(f32))
    xs, Bm, Cm = jnp.split(xbc, [D_S, D_S + S_GROUPS * S_STATE], axis=-1)
    xs = xs.reshape(B, S, S_HEADS, HEAD_DIM)
    rep = S_HEADS // S_GROUPS
    Bh = jnp.repeat(Bm.reshape(B, S, S_GROUPS, S_STATE), rep, axis=2)
    Ch = jnp.repeat(Cm.reshape(B, S, S_GROUPS, S_STATE), rep, axis=2)
    dt = jax.nn.softplus(dt_raw.astype(f32) + dt_bias.astype(f32))
    A = -jnp.exp(a_log.astype(f32))
    y = ssd_chunked(xs, dt, A, Bh, Ch) + d_skip.astype(f32)[:, None] * xs
    gated = y.reshape(B, S, D_S) * jax.nn.silu(z.astype(f32))
    out = rms_norm(gated.reshape(B, S, S_GROUPS, D_S // S_GROUPS), norm_w.reshape(S_GROUPS, -1))
    return out.reshape(B, S, D_S)

def hybrid_layer(x, positions, norm_w, w_in, gate_b, m_norm_w, conv_w, conv_b,
                 dt_bias, a_log, d_skip, s_norm_w, w_out, w_gate, w_up, w_down):
    B, S, _ = x.shape
    h = rms_norm(x, norm_w[0])
    proj = h @ w_in
    (mq, mk, mv, mo, mi, mf, aq, ak, av, iq, ik, iw, sz, sxbc, sdt) = jnp.split(proj, _split_points(), axis=-1)

    def heads(t, n):
        return t.reshape(B, S, n, -1)

    hm = mlstm_chunkwise(heads(mq, M_HEADS), heads(mk, M_HEADS), heads(mv, M_HEADS),
                         mi + gate_b[:M_HEADS], mf + gate_b[M_HEADS:])
    hm = rms_norm(hm, m_norm_w.reshape(M_HEADS, HEAD_DIM)).reshape(B, S, D_M)
    hm = (jax.nn.sigmoid(mo.astype(jnp.float32)) * hm).astype(x.dtype)

    aq_r = rope_partial(heads(aq, A_HEADS), positions)
    ak_r = rope_partial(heads(ak, A_HEADS), positions)
    iq_r = rope_partial(heads(iq, IDX_HEADS), positions)
    ik_r = rope_partial(ik[:, :, None, :], positions)[:, :, 0, :]
    ha = dsa_attention(aq_r, ak_r, heads(av, A_HEADS), iq_r, ik_r, iw * (IDX_HEADS ** -0.5))
    ha = ha.reshape(B, S, D_A).astype(x.dtype)

    hs = ssd_mixer(sxbc, sz, sdt, conv_w, conv_b, dt_bias, a_log, d_skip, s_norm_w).astype(x.dtype)

    mix = jnp.concatenate([hm, ha, hs], axis=-1) @ w_out
    x = x + rms_norm(mix, norm_w[1])
    h = rms_norm(x, norm_w[2])
    ff = (jax.nn.silu(h @ w_gate) * (h @ w_up)) @ w_down
    return x + rms_norm(ff, norm_w[3])

def setup_inputs(seed: int = 0) -> dict:
    key = jax.random.key(seed)
    ks = jax.random.split(key, 18)
    f32 = jnp.float32
    nrm = lambda k, shape, s: jax.random.normal(k, shape, f32) * s
    x = jax.random.normal(ks[0], (BATCH, SEQ, D_MODEL), f32)
    positions = jnp.broadcast_to(jnp.arange(SEQ, dtype=jnp.int32), (BATCH, SEQ))
    norm_w = 1.0 + nrm(ks[1], (DEPTH, 4, D_MODEL), 0.02)
    w_in = nrm(ks[2], (DEPTH, D_MODEL, N_IN), D_MODEL ** -0.5)
    i_bias = nrm(ks[3], (DEPTH, M_HEADS), 0.1)
    f_bias = jax.random.uniform(ks[4], (DEPTH, M_HEADS), f32, 3.0, 6.0)
    mlstm_gate_bias = jnp.concatenate([i_bias, f_bias], axis=-1)
    mlstm_norm_w = 1.0 + nrm(ks[5], (DEPTH, D_M), 0.02)
    conv_w = nrm(ks[6], (DEPTH, S_CONV, CONV_DIM), S_CONV ** -0.5)
    conv_b = nrm(ks[7], (DEPTH, CONV_DIM), 0.02)
    dt0 = jnp.exp(jax.random.uniform(ks[8], (DEPTH, S_HEADS), f32, math.log(1e-3), math.log(1e-1)))
    dt_bias = dt0 + jnp.log(-jnp.expm1(-dt0))
    a_log = jnp.log(jax.random.uniform(ks[9], (DEPTH, S_HEADS), f32, 1.0, 16.0))
    d_skip = 1.0 + nrm(ks[10], (DEPTH, S_HEADS), 0.1)
    ssd_norm_w = 1.0 + nrm(ks[11], (DEPTH, D_S), 0.02)
    w_out = nrm(ks[12], (DEPTH, D_MIX, D_MODEL), D_MIX ** -0.5)
    w_gate = nrm(ks[13], (DEPTH, D_MODEL, D_FF), D_MODEL ** -0.5)
    w_up = nrm(ks[14], (DEPTH, D_MODEL, D_FF), D_MODEL ** -0.5)
    w_down = nrm(ks[15], (DEPTH, D_FF, D_MODEL), D_FF ** -0.5)
    return {"x": x, "positions": positions, "norm_w": norm_w, "w_in": w_in,
            "mlstm_gate_bias": mlstm_gate_bias, "mlstm_norm_w": mlstm_norm_w,
            "conv_w": conv_w, "conv_b": conv_b, "dt_bias": dt_bias, "a_log": a_log,
            "d_skip": d_skip, "ssd_norm_w": ssd_norm_w, "w_out": w_out,
            "w_gate": w_gate, "w_up": w_up, "w_down": w_down}

def reference(x, positions, norm_w, w_in, mlstm_gate_bias, mlstm_norm_w, conv_w, conv_b,
              dt_bias, a_log, d_skip, ssd_norm_w, w_out, w_gate, w_up, w_down):
    for l in range(DEPTH):
        x = hybrid_layer(x, positions, norm_w[l], w_in[l], mlstm_gate_bias[l], mlstm_norm_w[l],
                         conv_w[l], conv_b[l], dt_bias[l], a_log[l], d_skip[l], ssd_norm_w[l],
                         w_out[l], w_gate[l], w_up[l], w_down[l])
    return x


_drawn_inputs = setup_inputs


def setup_inputs(seed=0):
    import zlib

    import numpy as np

    out = dict(_drawn_inputs(seed))
    spreads = {}
    factors = {}
    for name, (base, spread) in spreads.items():
        noise = np.random.default_rng([zlib.crc32(name.encode()), seed]).standard_normal(out[name].shape)
        drawn = base * np.exp(spread * noise) if base else spread * noise
        out[name] = __import__('jax').numpy.asarray(drawn.astype(out[name].dtype))
    for name, factor in factors.items():
        out[name] = (out[name] * factor).astype(out[name].dtype)
    return out
```

```python
from contextlib import ExitStack

import numpy as np

import concourse.bass as bass
from concourse import mybir

F32 = mybir.dt.float32
F32R = mybir.dt.float32r
I32 = mybir.dt.int32
ACT = mybir.ActivationFunctionType
ALU = mybir.AluOpType
AX = mybir.AxisListType

P = 128
D = 1024
S = 1024
DEPTH = 2
KT = D // P
NT = S // P
PLACES = 3
assert (NT - 2) % PLACES == 0
HALF = 512
HD = 64
MH = 4
AH = 4
SH = 8
SG = 2
DFF = 2816
FB = DFF // 256
TOPK = 256
EPS = 1e-6
ROUNDS_AT_A_TIME = 8
ATT_BESIDE = 24
NEG = -1e30
TAKEN = -3e38
TWO_PI_PARTS = (6.28125, 0.0019350051879882812, 3.0198e-07)

C_MQ, C_MK, C_MV, C_MO = 0, 256, 512, 768
C_MI, C_MF = 1024, 1028
C_AQ, C_AK, C_AV = 1032, 1288, 1544
C_IQ, C_IK, C_IW = 1800, 2056, 2120
C_SZ, C_XBC, C_DT = 2124, 2636, 3660
N_IN = 3668

U_SM, U_IK, U_IQ, U_AK, U_AV, U_AQ = 0, 1, 2, 4, 6, 8
U_XBC, U_SZ, U_MQ, U_MK, U_MV, U_MO = 10, 18, 22, 24, 26, 28
N_PROJ = 30
UNIT_COL = {}
for _u0, _c0, _n in ((U_IQ, C_IQ, 2), (U_AK, C_AK, 2), (U_AV, C_AV, 2), (U_AQ, C_AQ, 2), (U_XBC, C_XBC, 8),
                     (U_SZ, C_SZ, 4), (U_MQ, C_MQ, 2), (U_MK, C_MK, 2), (U_MV, C_MV, 2), (U_MO, C_MO, 2)):
    for _j in range(_n):
        UNIT_COL[_u0 + _j] = _c0 + P * _j
R_I, R_F, R_DT, R_IW = 0, 32, 64, 96
W_X, W_B, W_C, W_Z, W_MQ, W_MK, W_MV, W_MO = 0, 4, 6, 8, 12, 14, 16, 18
NW = 20
N_WOUT = KT
N_UNITS = N_PROJ + N_WOUT + 6 * FB

K_ID, K_TRI, K_NEG, K_ROT, K_SEL, K_PAIR, K_RST, K_FRQ = 0, 128, 256, 384, 512, 1536, 1792, 2816
N_CONST = 2817


class Signal:

    def __init__(self, sem, per_layer):
        self.sem, self.per_layer = sem, per_layer

    def __call__(self, layer, n):
        return self.sem, layer * self.per_layer + n


def constant_table():
    t = np.zeros((P, N_CONST), np.float32)
    r = np.arange(P)
    t[:, K_ID:K_ID + P] = np.eye(P)
    t[:, K_TRI:K_TRI + P] = r[None, :] >= r[:, None]
    t[:, K_NEG:K_NEG + P] = np.where(r[None, :] > r[:, None], NEG, 0.0)
    for m in range(P):
        d = m % HD
        if d < 8:
            t[m + 8, K_ROT + m] = -1.0
        elif d < 16:
            t[m - 8, K_ROT + m] = 1.0
    for h in range(8):
        t[h, K_SEL + P * h:K_SEL + P * (h + 1)] = 1.0
    for p in range(2):
        for m in range(P):
            t[2 * p + m // HD, K_PAIR + P * p + m] = 1.0
    t[:, K_RST:K_RST + S] = (np.arange(S) % P != 0)[None, :]
    d = r % HD
    freq = np.power(np.float32(500000.0), -(np.arange(8, dtype=np.float32) / np.float32(8)))
    t[:, K_FRQ] = np.where(d < 16, freq[d % 8], 0.0)
    return t


def build(nc, x, positions, norm_w, w_in, gate_b, m_norm_w, conv_w, conv_b, dt_bias, a_log, d_skip, s_norm_w,
          w_out, w_gate, w_up, w_down, table, out):
    rot = nc.dram_tensor("rot_scratch", [2, P, S], F32).ap()
    spill = nc.dram_tensor("proj_scratch", [NW, P, S], F32).ap()
    xmid = nc.dram_tensor("xmid_scratch", [S, D], F32).ap()

    ctx = ExitStack()
    with ctx:
        def sb(name, shape, dt=F32, stack=ctx):
            return stack.enter_context(nc.sbuf_tensor(name, shape, dt))

        def sig(name, per_layer):
            return Signal(ctx.enter_context(nc.semaphore(name)), per_layer)

        ps = ctx.enter_context(nc.psum_tensor("ps", [P, 8, HALF], F32))

        act_hi = sb("act_hi", [P, KT, S], F32R)
        act_lo = sb("act_lo", [P, KT, S], F32R)
        raw = [sb(f"raw{s}", [P, D]) for s in range(2)]
        whi = [sb(f"whi{s}", [P, D], F32R) for s in range(2)]
        wlo = [sb(f"wlo{s}", [P, D], F32R) for s in range(2)]
        cst = sb("cst", [P, N_CONST])
        ident = cst[:, K_ID:K_ID + P]
        nrow = [sb(f"nrow{s}", [P, D]) for s in range(2)]
        small = sb("small", [P, 64])
        dskip = sb("dskip", [P, SH])
        mnw = sb("mnw", [P, MH * HD])
        snw = sb("snw", [P, SH * HD])

        mix_mem = ExitStack()
        def mb(name, shape, dt=F32):
            return sb(name, shape, dt, mix_mem)
        width = [(c + 1) * P for c in range(NT)]
        sbase = [sum(width[:c]) for c in range(NT)]
        mrow = mb("mrow", [P, S])
        arow = mb("arow", [P, S])
        gcol = mb("gcol", [P, NT, 4, MH])
        scol = mb("scol", [P, NT, 4, SH])
        iwc = mb("iwc", [P, NT, AH])
        decm = mb("decm", [P, 2, NT])
        decs = mb("decs", [P, SH, NT])
        convc = mb("convc", [P, KT, 8])

        a_mem = ExitStack()
        def ab(name, shape, dt=F32):
            return sb(name, shape, dt, a_mem)
        score = ab("score", [P, sum(width)])
        ak = ab("ak", [P, 2, S])
        aq = ab("aq", [P, 2, S])
        avr = ab("avr", [P, NT, AH * HD])
        smw = ab("smw", [P, KT, P])
        stage = [ab(f"stage{s}", [P, 3 + S]) for s in range(2)]
        ik = ab("ik", [P, S])
        iq = ab("iq", [P, 2, S])
        smr = ab("smr", [P, S])
        cosf = ab("cosf", [P, S])
        sinf = ab("sinf", [P, S])
        tap = [ab(f"tap{k}", [P, S]) for k in range(4)]
        max8 = ab("max8", [P, 8])
        bcol = ab("bcol", [P, 4])
        cwr = ab("cwr", [8, KT * P])
        a_mem.close()


        b_mem = ExitStack()
        def bb(name, shape, dt=F32):
            return sb(name, shape, dt, b_mem)
        wc = [bb(f"wc{s}", [P, NW, P]) for s in range(PLACES)]
        rw = [bb(f"rw{s}", [P, 12, P]) for s in range(PLACES)]
        vaug = [bb(f"vaug{s}", [P, MH, HD + 1]) for s in range(PLACES)]
        pm = bb("pm", [P, MH, P])
        pss = bb("pss", [P, SH, P])
        xdt = bb("xdt", [P, SH, HD])
        xw = bb("xw", [P, SH, HD])
        wk = bb("wk", [P, MH, HD])
        y = bb("y", [P, SH, HD])
        nd = bb("nd", [P, MH, HD + 1])
        catr = bb("catr", [P, 768])
        catf = bb("catf", [P, 2, P])
        cmem = bb("cmem", [P, 2, 2, HD + 1])
        smem = bb("smem", [P, SH, HD])
        b_mem.close()


        mix_mem.close()

        d_mem = ExitStack()
        def db(name, shape, dt=F32):
            return sb(name, shape, dt, d_mem)
        wohi = db("wohi", [P, KT, D], F32R)
        wolo = db("wolo", [P, KT, D], F32R)
        wo_raw = [db(f"wo_raw{k}", [P, D]) for k in range(2, 6)]
        xres = [db(f"xres{s}", [P, D]) for s in range(2)]
        mixn = [db(f"mixn{s}", [P, D]) for s in range(2)]
        d_mem.close()


        e_mem = ExitStack()
        def eb(name, shape, dt=F32):
            return sb(name, shape, dt, e_mem)
        yacc = eb("yacc", [P, NT, D])
        hhi = [eb(f"hhi{s}", [P, 2, S], F32R) for s in range(2)]
        hlo = [eb(f"hlo{s}", [P, 2, S], F32R) for s in range(2)]
        dhi = [eb(f"dhi{s}", [P, D], F32R) for s in range(2)]
        dlo = [eb(f"dlo{s}", [P, D], F32R) for s in range(2)]
        sg = eb("sg", [P, S])
        hf = eb("hf", [P, S])
        own = [eb(f"resid{t}", [P, D]) for t in range(NT - 3)]
        e_mem.close()


        const_in = sig("const_in", 0)
        copied_x = sig("copied_x", 0)
        rot_step = sig("rot_step", 0)
        rot_act = sig("rot_act", 0)
        rot_out = sig("rot_out", 0)
        cleared = sig("cleared", 4)
        par_in = sig("par_in", 16 * 13)
        sm_in = sig("sm_in", 16 * 4)
        xa_in = [sig(f"xa_in{s}", 16 * 4) for s in range(2)]
        a_stat = sig("a_stat", 3 * NT)
        a_xn = sig("a_xn", NT)
        a_hi = sig("a_hi", NT)
        raw_in = [sig("raw_in0", 16 * 49), sig("raw_in1", 16 * 51)]
        w_hi = sig("w_hi", N_UNITS)
        w_lo = sig("w_lo", N_UNITS)
        pj = sig("pj", N_PROJ + 4 * FB)
        ev = sig("ev", N_PROJ)
        spilled = [sig(f"spilled{s}", 16 * 10) for s in range(2)]
        aux_names = ["cw"] + [("norm", t) for t in range(NT)] + ["iw", ("rope", 0), ("rope", 1),
                      ("rope", 2)]
        aux_names += [("idx", c, h) for c in range(NT) for h in range(AH)]
        aux_names += ["grow", "srow", "decay", ("rope", 3), ("rope", 4), ("av", 0), ("av", 1), ("rope", 5), ("rope", 6)]
        aux_at = {name: i for i, name in enumerate(aux_names)}
        n_aux = len(aux_names)
        aux_full = [sig(f"aux_full{s}", (n_aux + 1 - s) // 2) for s in range(2)]
        aux_free = [sig(f"aux_free{s}", (n_aux + 1 - s) // 2) for s in range(2)]
        bias_step = sig("bias_step", 1)
        rows_v = sig("rows_v", 24)
        rows_a = sig("rows_a", 9)
        act_fin = sig("act_fin", 2)
        rope_v = sig("rope_v", 3 * 3)
        rope_p = sig("rope_p", 3 * 4)
        acc = sig("acc", NT * AH)
        masked = sig("masked", NT)
        topk = sig("topk", 1)
        selected = sig("selected", NT - 2)
        taps = sig("taps", 4 * 8)
        conv = sig("conv", 3 * 8)
        csilu = sig("csilu", 8)

        sp_go = ctx.enter_context(nc.semaphore("sp_go"))

        def passed(sp):
            sp.sem_inc(sp_go, 1)

        def aux(name):
            i = aux_at[name]
            s = i % 2
            return s, i // 2, ps[:, 4 + 2 * s:6 + 2 * s, :].rearrange("p a b -> p (a b)")

        def copied(name):
            s, n, _ = aux(name)
            return aux_free[s](L, n + 1)

        def raw_wait(u):
            return 16 * (u // 2) if u % 2 == 0 else 16 * ((u + 1) // 2 + 1)

        def unit_psum(u):
            return ps[:, 2 * (u % 2):2 * (u % 2) + 2, :].rearrange("p a b -> p (a b)")

        def tiles(ap):
            return ap.rearrange("p (k n) -> p k n", n=P)

        w_in_v = w_in.rearrange("l (k p) n -> l p k n", p=P)

        with nc.Block() as block:
            @block.sync
            def _(sp):
                sp.dma_start(cst[:, :], table).then_inc(const_in.sem, 16)
                sp.dma_start(smr[:, :].bitcast(I32), positions.broadcast_to([P, S])).then_inc(const_in.sem, 16)
                sp.dma_start(out, x).then_inc(copied_x.sem, 16)
                sp.wait_ge(rot_act.sem, 2)
                sp.wait_ge(rot_step.sem, 9)
                sp.dma_start(rot[0], cosf[:, :]).then_inc(rot_out.sem, 16)
                sp.dma_start(rot[1], sinf[:, :]).then_inc(rot_out.sem, 16)
                sp.wait_ge(rot_out.sem, 32)
                sp.wait_ge(copied_x.sem, 16)

            @block.vector
            def _(v):
                ang, turns, half = tap[0], tap[1], tap[2]
                v.wait_ge(const_in.sem, 32)
                v.tensor_copy(ang[:, :], smr[:, :].bitcast(I32)).then_inc(rot_step.sem, 1)
                v.wait_ge(rot_step.sem, 1)
                v.tensor_scalar(ang[:, :], ang[:, :], cst[:, K_FRQ:K_FRQ + 1], None, ALU.mult).then_inc(rot_step.sem, 1)
                v.wait_ge(rot_step.sem, 2)
                v.tensor_scalar(turns[:, :], ang[:, :], float(1 / (2 * np.pi)), 12582912.0, ALU.mult, ALU.add).then_inc(rot_step.sem, 1)
                v.wait_ge(rot_step.sem, 3)
                v.tensor_scalar(turns[:, :], turns[:, :], 12582912.0, None, ALU.subtract).then_inc(rot_step.sem, 1)
                for i, part in enumerate(TWO_PI_PARTS):
                    v.wait_ge(rot_step.sem, 4 + i)
                    v.scalar_tensor_tensor(out=ang[:, :], in0=turns[:, :], scalar=-part, in1=ang[:, :],
                                           op0=ALU.mult, op1=ALU.add).then_inc(rot_step.sem, 1)
                v.wait_ge(rot_step.sem, 7)
                v.tensor_scalar(ang[:, :], ang[:, :], 3.1415925, -3.1415925, ALU.min, ALU.max).then_inc(rot_step.sem, 1)
                v.wait_ge(rot_act.sem, 3)
                v.tensor_scalar(cosf[:, :], half[:, :], -2.0, 1.0, ALU.mult, ALU.add).then_inc(rot_step.sem, 1)

            @block.scalar
            def _(act):
                act.wait_ge(rot_step.sem, 8)
                act.activation(sinf[:, :], tap[0][:, :], ACT.Sin).then_inc(rot_act.sem, 1)
                act.activation(tap[2][:, :], tap[0][:, :], ACT.Sin, scale=0.5).then_inc(rot_act.sem, 1)
                act.wait_ge(rot_act.sem, 2)
                act.activation(tap[2][:, :], tap[2][:, :], ACT.Square).then_inc(rot_act.sem, 1)

        L = ctx.enter_context(nc.Fori(0, DEPTH))

        rope_tiles = [(U_IK, ik[:, :]), (U_IQ, iq[:, 0]), (U_IQ + 1, iq[:, 1]), (U_AK, ak[:, 0]), (U_AK + 1, ak[:, 1]),
                      (U_AQ, aq[:, 0]), (U_AQ + 1, aq[:, 1])]
        rope_of = {u: i for i, (u, _) in enumerate(rope_tiles)}
        rows_t = [ak[:, 0], ak[:, 1], aq[:, 0], aq[:, 1]]
        dec_row, mprev, al_row = small[0:MH, 8:16], small[0:MH, 16:24], small[0:SH, 24:32]
        row = lambda l, a: a[bass.ds(l, 1)]
        heads = lambda a, n: a.rearrange("p (h n) -> p h n", n=n)
        lg, pt, oatt = [iq[:, 0], iq[:, 1]], [ik, smr], [cosf[:, 0:AH * HD], cosf[:, AH * HD:2 * AH * HD]]
        mx, nb, sm_, rs = 32, 36, 40, 48
        N_PAIRS = NT * AH
        c_clear = sig("c_clear", 4)
        c_qk = sig("c_qk", N_PAIRS)
        c_max = sig("c_max", N_PAIRS)
        c_bias = sig("c_bias", N_PAIRS)
        c_exp = sig("c_exp", N_PAIRS)
        c_turn = sig("c_turn", N_PAIRS)
        c_pt = sig("c_pt", N_PAIRS)
        c_pv = sig("c_pv", N_PAIRS)
        c_out = sig("c_out", 2 * NT)
        c_cat = sig("c_cat", NT)
        c_hi = sig("c_hi", NT)
        c_lo = sig("c_lo", NT)


        with nc.Block() as block:
            @block.sync
            def _(sp):
                def x_tile(t):
                    if t >= 2:
                        sp.wait_ge(*aux_full[aux(("norm", t - 2))[0]](L, aux(("norm", t - 2))[1] + 1))
                    sp.dma_start(tap[t % 2][:, :], out[t * P:(t + 1) * P, :]).then_inc(xa_in[t % 2].sem, 16)

                def unit(u):
                    if u >= 3:
                        sp.wait_ge(*w_lo(L, u - 1))
                        passed(sp)
                    dst = tiles(raw[u % 2][:, :])
                    if u == U_IK:
                        for j in range(2):
                            sp.dma_start(dst[:, :, HD * j:HD * (j + 1)], row(L, w_in_v)[0, :, :, C_IK:C_IK + HD])\
                              .then_inc(raw_in[u % 2].sem, 16)
                    else:
                        c0 = UNIT_COL[u]
                        sp.dma_start(dst, row(L, w_in_v)[0, :, :, c0:c0 + P]).then_inc(raw_in[u % 2].sem, 16)

                x_tile(0)
                x_tile(1)
                sp.dma_start(nrow[0][:, :], row(L, norm_w)[:, 0].broadcast_to([P, D])).then_inc(par_in.sem, 16)
                sp.wait_ge(*cleared(L, 4))
                passed(sp)
                for c0, n, r in ((C_MI, MH, R_I), (C_MF, MH, R_F), (C_DT, SH, R_DT), (C_IW, AH, R_IW)):
                    sp.dma_start(smw[:, :, r:r + n], row(L, w_in_v)[0, :, :, c0:c0 + n]).then_inc(sm_in.sem, 16)
                col = lambda a: a.rearrange("o n -> n o")
                sp.dma_start(bcol[R_I:R_I + MH, 0:1], col(row(L, gate_b)[:, 0:MH])).then_inc(par_in.sem, 16)
                sp.dma_start(bcol[R_F:R_F + MH, 0:1], col(row(L, gate_b)[:, MH:2 * MH])).then_inc(par_in.sem, 16)
                sp.dma_start(bcol[R_DT:R_DT + SH, 0:1], col(row(L, dt_bias))).then_inc(par_in.sem, 16)
                sp.dma_start(bcol[0:SH, 1:2], col(row(L, a_log))).then_inc(par_in.sem, 16)
                sp.dma_start(cwr[0:4, :], row(L, conv_w)[0]).then_inc(par_in.sem, 16)
                sp.dma_start(cwr[4:5, :], row(L, conv_b)).then_inc(par_in.sem, 16)
                sp.dma_start(dskip[:, :], row(L, d_skip).broadcast_to([P, SH])).then_inc(par_in.sem, 16)
                sp.dma_start(mnw[:, :], row(L, m_norm_w).broadcast_to([P, MH * HD])).then_inc(par_in.sem, 16)
                sp.dma_start(snw[:, :], row(L, s_norm_w).broadcast_to([P, SH * HD])).then_inc(par_in.sem, 16)
                sp.dma_start(cosf[:, :], rot[0]).then_inc(par_in.sem, 16)
                sp.dma_start(sinf[:, :], rot[1]).then_inc(par_in.sem, 16)
                sp.dma_start(cwr[5:8, :], row(L, conv_w)[0, 0:3]).then_inc(par_in.sem, 16)
                unit(1)
                unit(2)
                for t in range(2, NT):
                    x_tile(t)
                for u in range(3, N_PROJ):
                    unit(u)

            @block.gpsimd
            def _(pool):
                pool.memset(smw[:, :, :], 0.0).then_inc(cleared.sem, 1)
                pool.memset(bcol[:, :], 0.0).then_inc(cleared.sem, 1)
                pool.memset(stage[0][:, 0:3], 0.0).then_inc(cleared.sem, 1)
                pool.memset(stage[1][:, 0:3], 0.0).then_inc(cleared.sem, 1)

                def lo(u):
                    pool.wait_ge(*w_hi(L, u + 1))
                    src = smw[:, :, :].rearrange("p k n -> p (k n)") if u == 0 else raw[u % 2][:, :]
                    pool.tensor_tensor(wlo[u % 2][:, :], src, whi[u % 2][:, :].bitcast(F32), ALU.subtract)\
                        .then_inc(w_lo.sem, 1)

                def rotate(i):
                    u, dst = rope_tiles[i]
                    n = 3 * (i - 3)
                    if i == 3:
                        pool.wait_ge(*rows_v(L, 24))
                    pool.wait_ge(*ev(L, u + 1))
                    pool.tensor_tensor(dst, stage[u % 2][:, 3:], cosf[:, :], ALU.mult).then_inc(rope_p.sem, 1)
                    pool.wait_ge(*copied(("rope", i)))
                    pool.tensor_tensor(tap[3][:, :], tap[3][:, :], sinf[:, :], ALU.mult).then_inc(rope_p.sem, 1)
                    pool.wait_ge(*rope_p(L, n + 2))
                    pool.tensor_tensor(dst, dst, tap[3][:, :], ALU.add).then_inc(rope_p.sem, 1)

                def conv_sum(j):
                    pool.wait_ge(*taps(L, 4 * j + 4))
                    pool.tensor_tensor(tap[0][:, :], tap[0][:, :], tap[1][:, :], ALU.add).then_inc(conv.sem, 1)
                    pool.tensor_tensor(tap[2][:, :], tap[2][:, :], tap[3][:, :], ALU.add).then_inc(conv.sem, 1)
                    pool.wait_ge(*conv(L, 3 * j + 2))
                    pool.tensor_tensor(tap[0][:, :], tap[0][:, :], tap[2][:, :], ALU.add).then_inc(conv.sem, 1)

                lo(0)
                lo(1)
                for u in range(N_PROJ):
                    if u + 2 < N_PROJ:
                        lo(u + 2)
                    if u in rope_of and rope_of[u] >= 3:
                        rotate(rope_of[u])
                    if U_XBC <= u < U_XBC + 8:
                        conv_sum(u - U_XBC)

            @block.scalar
            def _(act):
                def hi(u):
                    if u == 0:
                        act.wait_ge(*sm_in(L, 64))
                        src = smw[:, :, :].rearrange("p k n -> p (k n)")
                    else:
                        act.wait_ge(*raw_in[u % 2](L, raw_wait(u)))
                        src = raw[u % 2][:, :]
                    if u >= 2:
                        act.wait_ge(*pj(L, u - 1))
                    act.activation(whi[u % 2][:, :], src, ACT.Copy).then_inc(w_hi.sem, 1)

                def stat(t):
                    s = 4 * (t % 2)
                    act.wait_ge(*xa_in[t % 2](L, 16 * (t // 2 + 1)))
                    if t >= 2:
                        act.wait_ge(*a_xn(L, t - 1))
                    act.activation(tap[2][:, :], tap[t % 2][:, :], ACT.Square, accum_out=small[:, s:s + 1]).then_inc(a_stat.sem, 1)
                    act.wait_ge(*a_stat(L, 3 * t + 1))
                    act.activation(small[:, s + 1:s + 2], small[:, s:s + 1], ACT.Ln, bias=EPS, scale=1.0 / D).then_inc(a_stat.sem, 1)
                    act.wait_ge(*a_stat(L, 3 * t + 2))
                    act.activation(small[:, s + 2:s + 3], small[:, s + 1:s + 2], ACT.Exp, scale=-0.5).then_inc(a_stat.sem, 1)

                def norm_hi(t):
                    s, n, bank = aux(("norm", t))
                    act.wait_ge(*aux_full[s](L, n + 1))
                    act.activation(act_hi[:, :, t * P:(t + 1) * P], tiles(bank), ACT.Copy).then_inc(a_hi.sem, 1)

                def evac(u):
                    act.wait_ge(*pj(L, u + 1))
                    if u == U_SM:
                        act.wait_ge(*par_in(L, 16 * 13))
                        act.activation(smr[:, :], unit_psum(u), ACT.Identity, bias=bcol[:, 0:1]).then_inc(ev.sem, 1)
                        return
                    v = u - 2
                    if v in rope_of:
                        i = rope_of[v]
                        act.wait_ge(*(rope_v(L, 3 * i + 3) if i < 3 else rope_p(L, 3 * (i - 3) + 3)))
                    elif v in (U_AV, U_AV + 1):
                        s, n, _ = aux(("av", v - U_AV))
                        act.wait_ge(*aux_full[s](L, n + 1))
                    elif v >= U_XBC:
                        act.wait_ge(*spilled[v % 2](L, 16 * ((v - U_XBC) // 2 + 1)))
                    f = ACT.Copy
                    k = 1.0
                    if U_SZ <= u < U_SZ + 4:
                        f = ACT.Silu
                    if U_MO <= u < U_MO + 2:
                        f = ACT.Sigmoid
                    if U_MK <= u < U_MK + 2:
                        k = HD ** -0.5
                    act.activation(stage[u % 2][:, 3:], unit_psum(u), f, scale=k).then_inc(ev.sem, 1)

                def rope_copy(i):
                    s, n, bank = aux(("rope", i))
                    act.wait_ge(*aux_full[s](L, n + 1))
                    if i >= 1:
                        act.wait_ge(*(rope_v(L, 3 * i) if i <= 3 else rope_p(L, 3 * (i - 3))))
                    act.activation(tap[3][:, :], bank, ACT.Copy).then_inc(aux_free[s].sem, 1)

                def columns(name, dst, src):
                    s, n, bank = aux(name)
                    act.wait_ge(*aux_full[s](L, n + 1))
                    act.activation(dst, src(bank), ACT.Copy).then_inc(aux_free[s].sem, 1)

                def spill_unit(u):
                    j = u - U_XBC
                    act.dma_start(spill[j], stage[u % 2][:, 3:]).then_inc(spilled[u % 2].sem, 16)

                def conv_silu(u):
                    act.wait_ge(*conv(L, 3 * (u - U_XBC) + 3))
                    act.activation(stage[u % 2][:, 3:], tap[0][:, :], ACT.Silu).then_inc(csilu.sem, 1)
                    act.wait_ge(*csilu(L, u - U_XBC + 1))
                    spill_unit(u)

                def conv_taps(u):
                    act.wait_ge(*ev(L, u + 1))
                    if u == U_XBC:
                        act.wait_ge(*copied("cw"))
                        act.wait_ge(*rope_p(L, 12))
                        act.wait_ge(*acc(L, NT * AH))
                    for k in range(4):
                        act.activation(tap[k][:, :], stage[u % 2][:, k:k + S], ACT.Identity,
                                       bias=convc[:, u - U_XBC, 4:5] if k == 3 else 0.0,
                                       scale=convc[:, u - U_XBC, k:k + 1]).then_inc(taps.sem, 1)

                act.preload_act_table_set("natural_log_exp_and_others")
                columns("cw", convc[:, :, :], lambda b: b[:, 0:64].rearrange("p (k n) -> p k n", n=8))
                act.wait_ge(*par_in(L, 16 * 13))
                act.activation(bcol[0:SH, 2:3], bcol[0:SH, 1:2], ACT.Exp).then_inc(bias_step.sem, 1)
                hi(0)
                hi(1)
                for t in range(NT + 1):
                    if t < NT:
                        stat(t)
                    if t >= 1:
                        norm_hi(t - 1)
                evac(0)
                hi(2)
                t0, t1, t2, t3 = rows_t
                act.wait_ge(*rows_v(L, 1))
                act.activation(t0, t0, ACT.Exp, scale=-1.0).then_inc(rows_a.sem, 1)
                act.wait_ge(*rows_v(L, 2))
                act.activation(t2, t1, ACT.Ln).then_inc(rows_a.sem, 1)
                evac(1)
                hi(3)
                columns("iw", iwc[:, :, :], lambda b: tiles(b)[:, :, R_IW:R_IW + AH])
                act.wait_ge(*rows_v(L, 16))
                act.activation(t1[32:36], t1[32:36], ACT.Exp).then_inc(rows_a.sem, 1)
                act.activation(t1[64:68], t1[64:68], ACT.Exp).then_inc(rows_a.sem, 1)
                act.activation(t1[96:100], t1[96:100], ACT.Exp, scale=-1.0).then_inc(rows_a.sem, 1)
                act.activation(dec_row, dec_row, ACT.Exp).then_inc(rows_a.sem, 1)
                act.wait_ge(*rows_v(L, 22))
                act.activation(t3[0:SH], t3[0:SH], ACT.Exp).then_inc(rows_a.sem, 1)
                act.activation(t2[32:40], arow[0:SH], ACT.Exp).then_inc(rows_a.sem, 1)
                act.activation(al_row, arow[0:SH, P - 1::P], ACT.Exp).then_inc(rows_a.sem, 1)
                evac(2)
                hi(4)
                rope_copy(0)
                evac(3)
                hi(5)
                rope_copy(1)
                evac(4)
                hi(6)
                rope_copy(2)
                for c in range(NT):
                    for h in range(AH):
                        m = c * AH + h
                        s, n, bank = aux(("idx", c, h))
                        act.wait_ge(*aux_full[s](L, n + 1))
                        if m >= 2:
                            act.wait_ge(*acc(L, m - 1))
                        act.activation(tap[m % 2][:, 0:width[c]], bank[:, 0:width[c]], ACT.Relu)\
                           .then_inc(aux_free[s].sem, 1)
                columns("grow", gcol[:, :, :, :],
                        lambda b: b.rearrange("p (c q r) -> p c q r", q=4, r=32)[:, :, :, 0:MH])
                columns("srow", scol[:, :, :, :],
                        lambda b: b.rearrange("p (c q r) -> p c q r", q=4, r=32)[:, :, :, 0:SH])
                s, n, bank = aux("decay")
                act.wait_ge(*aux_full[s](L, n + 1))
                act.activation(decm[:, :, :], bank[:, 0:16].rearrange("p (k n) -> p k n", n=NT), ACT.Copy)
                act.activation(decs[:, :, :], bank[:, 16:80].rearrange("p (k n) -> p k n", n=NT), ACT.Copy)\
                   .then_inc(aux_free[s].sem, 1)
                for u in range(5, N_PROJ):
                    evac(u)
                    if u + 2 < N_PROJ:
                        hi(u + 2)
                    if u - 1 in rope_of and u >= 5:
                        rope_copy(rope_of[u - 1])
                    if u - 1 in (U_AV, U_AV + 1):
                        j = u - 1 - U_AV
                        columns(("av", j), avr[:, :, P * j:P * (j + 1)], tiles)
                    if U_XBC <= u - 1 < U_XBC + 8:
                        conv_silu(u - 1)
                    if U_XBC <= u < U_XBC + 8:
                        conv_taps(u)
                    if u >= U_SZ:
                        act.wait_ge(*ev(L, u + 1))
                        spill_unit(u)
                def exps(m):
                    c, h = divmod(m, AH)
                    act.wait_ge(*c_bias(L, m + 1))
                    if h == 0 and c >= 2:
                        act.wait_ge(*c_out(L, 2 * (c - 2) + 1))
                    act.activation(lg[m % 2][:, 0:width[c]], lg[m % 2][:, 0:width[c]], ACT.Exp,
                                   bias=small[:, nb + m % 2:nb + m % 2 + 1], scale=HD ** -0.5,
                                   accum_out=small[:, sm_ + AH * (c % 2) + h:sm_ + AH * (c % 2) + h + 1]).then_inc(c_exp.sem, 1)

                def hi_rows(c):
                    act.wait_ge(*c_cat(L, c + 1))
                    act.activation(act_hi[:, 2:4, c * P:(c + 1) * P], ps[:, 6 + c % 2, 256:512].rearrange("p (k n) -> p k n", n=P),
                                   ACT.Copy).then_inc(c_hi.sem, 1)

                exps(0)
                exps(1)
                for m in range(N_PAIRS):
                    c, h = divmod(m, AH)
                    act.wait_ge(*c_turn(L, m + 1))
                    if m >= 2:
                        act.wait_ge(*c_pv(L, m - 1))
                    act.activation(pt[m % 2][:, 0:width[c]], ps[:, 4:6, :].rearrange("p a b -> p (a b)")[:, 0:width[c]],
                                   ACT.Copy).then_inc(c_pt.sem, 1)
                    if h == 1 and c >= 1:
                        hi_rows(c - 1)
                    if m + 2 < N_PAIRS:
                        exps(m + 2)
                hi_rows(NT - 1)
                for s in range(2):
                    act.wait_ge(*spilled[s](L, 160))
                    act.sem_inc(act_fin.sem, 1)

            @block.tensor
            def _(pe):
                def project(u, s):
                    pe.wait_ge(*w_lo(L, u + 1))
                    if not (isinstance(u, int) and u < 2):
                        pe.wait_ge(*ev(L, u - 1))
                    wh, wl = tiles(whi[s][:, :]), tiles(wlo[s][:, :])
                    for half in range(2):
                        cols = slice(half * HALF, (half + 1) * HALF)
                        for k in range(KT):
                            for m, (w, a) in enumerate(((wh, act_hi), (wh, act_lo), (wl, act_hi))):
                                mm = pe.matmul(ps[:, 2 * s + half, :], w[:, k], a[:, k, cols],
                                               start=(k == 0 and m == 0), stop=(k == KT - 1 and m == 2))
                    mm.then_inc(pj.sem, 1)

                def take(name):
                    s, n, bank = aux(name)
                    if n >= 1:
                        pe.wait_ge(*aux_free[s](L, n))
                    return s, bank

                def swap_halves(i):
                    u, _ = rope_tiles[i]
                    s, bank = take(("rope", i))
                    pe.wait_ge(*ev(L, u + 1))
                    for half in range(2):
                        mm = pe.matmul(ps[:, 4 + 2 * s + half, :], cst[:, K_ROT:K_ROT + P],
                                       stage[u % 2][:, 3 + half * HALF:3 + (half + 1) * HALF], start=True, stop=True)
                    mm.then_inc(aux_full[s].sem, 1)

                def turn(name, src):
                    s, bank = take(name)
                    for j in range(NT):
                        mm = pe.transpose(tiles(bank)[:, j], src[:, j * P:(j + 1) * P], ident)
                    mm.then_inc(aux_full[s].sem, 1)

                s, bank = take("cw")
                pe.wait_ge(*par_in(L, 16 * 13))
                for j in range(KT):
                    mm = pe.matmul(bank[:, 8 * j:8 * j + 8], cwr[0:8, j * P:(j + 1) * P], ident[0:8, 0:8], start=True, stop=True)
                mm.then_inc(aux_full[s].sem, 1)
                for t in range(NT):
                    pe.wait_ge(*a_xn(L, t + 1))
                    turn(("norm", t), tap[t % 2][:, :])
                pe.wait_ge(*copied(("norm", NT - 1)))
                pe.wait_ge(*copied(("norm", NT - 2)))
                project(0, 0)
                project(1, 1)
                pe.wait_ge(*ev(L, 1))
                turn("iw", smr[:, :])
                project(2, 0)
                swap_halves(0)
                project(3, 1)
                swap_halves(1)
                project(4, 0)
                swap_halves(2)
                pe.wait_ge(*rope_v(L, 9))
                for c in range(NT):
                    for h in range(AH):
                        s, bank = take(("idx", c, h))
                        q0 = HD * (h % 2)
                        for b0 in range(0, width[c], HALF):
                            b1 = min(b0 + HALF, width[c])
                            mm = pe.matmul(bank[:, b0:b1], iq[q0:q0 + HD, h // 2, c * P:(c + 1) * P],
                                           ik[q0:q0 + HD, b0:b1], start=True, stop=True)
                        mm.then_inc(aux_full[s].sem, 1)
                pe.wait_ge(*rows_v(L, 24))
                pe.wait_ge(*rows_a(L, 9))
                turn("grow", rows_t[1])
                turn("srow", rows_t[2])
                s, bank = take("decay")
                for p in range(2):
                    pe.matmul(bank[:, 8 * p:8 * p + 8], cst[0:MH, K_PAIR + P * p:K_PAIR + P * (p + 1)], dec_row,
                              start=True, stop=True)
                for h in range(SH):
                    mm = pe.matmul(bank[:, 16 + 8 * h:24 + 8 * h], cst[0:SH, K_SEL + P * h:K_SEL + P * (h + 1)], al_row,
                                   start=True, stop=True)
                mm.then_inc(aux_full[s].sem, 1)
                for u in range(5, 12):
                    project(u, u % 2)
                    if u - 1 in rope_of:
                        swap_halves(rope_of[u - 1])
                    if u - 1 in (U_AV, U_AV + 1):
                        pe.wait_ge(*ev(L, u))
                        turn(("av", u - 1 - U_AV), stage[(u - 1) % 2][:, 3:])
                with pe.Fori(12, N_PROJ, 2) as u:
                    for s in range(2):
                        project(u + s, s)

                def logits(m):
                    c, h = divmod(m, AH)
                    q = slice(HD * (h % 2), HD * (h % 2) + HD)
                    if m >= 2:
                        pe.wait_ge(*c_max(L, m - 1))
                    for b0 in range(0, width[c], HALF):
                        b1 = min(b0 + HALF, width[c])
                        mm = pe.matmul(unit_psum(m)[:, b0:b1], aq[q, h // 2, c * P:(c + 1) * P], ak[q, h // 2, b0:b1],
                                       start=True, stop=True)
                    mm.then_inc(c_qk.sem, 1)

                def cat_turn(c):
                    pe.wait_ge(*c_out(L, 2 * c + 2))
                    for i in range(2):
                        mm = pe.transpose(ps[:, 6 + c % 2, 256 + i * P:256 + (i + 1) * P], oatt[c % 2][:, i * P:(i + 1) * P], ident)
                    mm.then_inc(c_cat.sem, 1)

                pe.wait_ge(*ev(L, N_PROJ))
                pe.wait_ge(*copied(aux_names[-1]))
                pe.wait_ge(*copied(aux_names[-2]))
                logits(0)
                logits(1)
                for m in range(N_PAIRS):
                    c, h = divmod(m, AH)
                    pe.wait_ge(*c_exp(L, m + 1))
                    if m >= 1:
                        pe.wait_ge(*c_pt(L, m))
                    for j in range(c + 1):
                        mm = pe.transpose(ps[:, 4 + j // 4, (j % 4) * P:(j % 4 + 1) * P], lg[m % 2][:, j * P:(j + 1) * P], ident)
                    mm.then_inc(c_turn.sem, 1)
                    if m + 2 < N_PAIRS:
                        logits(m + 2)
                    pe.wait_ge(*c_pt(L, m + 1))
                    if h == 0 and c >= 2:
                        pe.wait_ge(*c_lo(L, c - 1))
                    for j in range(c + 1):
                        mm = pe.matmul(ps[:, 6 + c % 2, HD * h:HD * (h + 1)], pt[m % 2][:, j * P:(j + 1) * P],
                                       avr[:, j, HD * h:HD * (h + 1)], start=(j == 0), stop=(j == c))
                    mm.then_inc(c_pv.sem, 1)
                    if h == 0 and c >= 1:
                        cat_turn(c - 1)
                cat_turn(NT - 1)

            @block.vector
            def _(v):
                v.wait_ge(*par_in(L, 16 * 13))

                def normalise(t):
                    v.wait_ge(*a_stat(L, 3 * t + 3))
                    v.scalar_tensor_tensor(out=tap[t % 2][:, :], in0=tap[t % 2][:, :],
                                           scalar=small[:, 4 * (t % 2) + 2:4 * (t % 2) + 3], in1=nrow[0][:, :],
                                           op0=ALU.mult, op1=ALU.mult).then_inc(a_xn.sem, 1)

                def norm_lo(t):
                    s, n, bank = aux(("norm", t))
                    v.wait_ge(*a_hi(L, t + 1))
                    v.tensor_tensor(act_lo[:, :, t * P:(t + 1) * P], tiles(bank),
                                    act_hi[:, :, t * P:(t + 1) * P].bitcast(F32), ALU.subtract)\
                     .then_inc(aux_free[s].sem, 1)

                for t in range(NT + 1):
                    if t < NT:
                        normalise(t)
                    if t >= 1:
                        norm_lo(t - 1)

                t0, t1, t2, t3 = rows_t
                step = [0]

                def then(ins):
                    ins.then_inc(rows_v.sem, 1)
                    step[0] += 1
                    v.wait_ge(*rows_v(L, step[0]))

                chunks = lambda a: a.rearrange("p (c t) -> p c t", t=P)
                last = lambda a: a.rearrange("p (c t) -> p c t", t=P)[:, :, P - 1:P]
                v.wait_ge(*ev(L, 1))
                then(v.scalar_tensor_tensor(out=t0, in0=smr[:, :], scalar=-1.0, in1=smr[:, :], op0=ALU.mult, op1=ALU.max))
                v.wait_ge(*rows_a(L, 1))
                then(v.tensor_scalar(t1, t0, 1.0, None, ALU.add))
                v.wait_ge(*rows_a(L, 2))
                then(v.scalar_tensor_tensor(out=t1, in0=t1, scalar=1.0, in1=t0, op0=ALU.subtract, op1=ALU.subtract))
                then(v.tensor_tensor(t2, t2, t1, ALU.subtract))
                then(v.scalar_tensor_tensor(out=t3[0:MH], in0=smr[R_F:R_F + MH, :], scalar=0.0, in1=t2[R_F:R_F + MH],
                                            op0=ALU.min, op1=ALU.subtract))
                then(v.tensor_tensor_scan(t0[0:MH], cst[0:MH, K_RST:K_RST + S], t3[0:MH], 0.0, ALU.mult, ALU.add))
                then(v.memset(t1, 0.0))
                then(v.tensor_tensor(t1[0:MH], smr[0:MH, :], t0[0:MH], ALU.subtract))
                then(v.memset(t3, 0.0))
                then(v.tensor_copy(chunks(t3[0:MH])[:, 1:NT, 0:1], last(t0[0:MH])[:, 0:NT - 1]))
                then(v.tensor_tensor_scan(mrow[0:MH, :], t3[0:MH], t1[0:MH], 0.0, ALU.add, ALU.max))
                v.memset(mprev[:, 0:1], 0.0)
                then(v.tensor_tensor(mprev[:, 1:NT].rearrange("p (c o) -> p c o", o=1), last(t0[0:MH])[:, 0:NT - 1],
                                     last(mrow[0:MH, :])[:, 0:NT - 1], ALU.add))
                mlast = last(mrow[0:MH, :]).broadcast_to([MH, NT, P])
                then(v.tensor_tensor(chunks(t1[32:36]), mprev.rearrange("p (c o) -> p c o", o=1).broadcast_to([MH, NT, P]),
                                     chunks(mrow[0:MH, :]), ALU.subtract))
                then(v.tensor_tensor(chunks(t1[64:68]), chunks(t1[0:MH]), mlast, ALU.subtract))
                then(v.tensor_tensor(t1[96:100], t0[0:MH], mrow[0:MH, :], ALU.add))
                then(v.tensor_tensor(dec_row.rearrange("p (c o) -> p c o", o=1), mprev.rearrange("p (c o) -> p c o", o=1),
                                     last(mrow[0:MH, :]), ALU.subtract))
                then(v.scalar_tensor_tensor(out=t0[0:SH], in0=smr[R_DT:R_DT + SH, :], scalar=0.0, in1=t2[R_DT:R_DT + SH],
                                            op0=ALU.max, op1=ALU.add))
                v.wait_ge(*bias_step(L, 1))
                then(v.tensor_scalar(t3[0:SH], t0[0:SH], bcol[0:SH, 2:3], -1.0, ALU.mult, ALU.mult))
                then(v.tensor_tensor_scan(arow[0:SH, :], cst[0:SH, K_RST:K_RST + S], t3[0:SH], 0.0, ALU.mult, ALU.add))
                then(v.memset(t2, 0.0))
                then(v.tensor_copy(t2[0:SH], arow[0:SH, :]))
                then(v.tensor_tensor(chunks(t3[0:SH]), last(arow[0:SH, :]).broadcast_to([SH, NT, P]),
                                     chunks(arow[0:SH, :]), ALU.subtract))
                v.wait_ge(*rows_a(L, 7))
                then(v.tensor_tensor(t2[64:72], t3[0:SH], t0[0:SH], ALU.mult))
                then(v.tensor_copy(t2[96:104], t0[0:SH]))
                assert step[0] == 24

                for i in range(3):
                    u, dst = rope_tiles[i]
                    v.wait_ge(*ev(L, u + 1))
                    v.tensor_tensor(dst, stage[u % 2][:, 3:], cosf[:, :], ALU.mult).then_inc(rope_v.sem, 1)
                    v.wait_ge(*copied(("rope", i)))
                    v.tensor_tensor(tap[3][:, :], tap[3][:, :], sinf[:, :], ALU.mult).then_inc(rope_v.sem, 1)
                    v.wait_ge(*rope_v(L, 3 * i + 2))
                    v.tensor_tensor(dst, dst, tap[3][:, :], ALU.add).then_inc(rope_v.sem, 1)

                v.wait_ge(*copied("iw"))
                for c in range(NT):
                    sc = score[:, sbase[c]:sbase[c] + width[c]]
                    for h in range(AH):
                        m = c * AH + h
                        v.wait_ge(*copied(("idx", c, h)))
                        src = tap[m % 2][:, 0:width[c]]
                        if h == 0:
                            v.tensor_scalar(sc, src, iwc[:, c, 0:1], None, ALU.mult).then_inc(acc.sem, 1)
                        else:
                            v.wait_ge(*acc(L, m))
                            v.scalar_tensor_tensor(out=sc, in0=src, scalar=iwc[:, c, h:h + 1], in1=sc,
                                                   op0=ALU.mult, op1=ALU.add).then_inc(acc.sem, 1)
                for c in range(NT):
                    diag = score[:, sbase[c] + c * P:sbase[c] + width[c]]
                    v.wait_ge(*acc(L, (c + 1) * AH))
                    v.tensor_tensor(diag, diag, cst[:, K_NEG:K_NEG + P], ALU.add).then_inc(masked.sem, 1)
                v.wait_ge(*masked(L, NT))
                for c in range(2):
                    n = score[:, sbase[c]:sbase[c] + width[c]]
                    v.memset(n, 0.0).then_inc(c_clear.sem, 1)
                    v.wait_ge(*c_clear(L, 2 * c + 1))
                    v.tensor_copy(n[:, c * P:], cst[:, K_NEG:K_NEG + P]).then_inc(c_clear.sem, 1)
                v.wait_ge(*c_clear(L, 4))

                def maximum(m):
                    c, h = divmod(m, AH)
                    if h == 0 and c >= 2:
                        v.wait_ge(*selected(L, c - 1))
                    v.wait_ge(*c_qk(L, m + 1))
                    if m >= 2:
                        v.wait_ge(*c_turn(L, m - 1))
                    v.memset(small[:, 61:62], 0.0)
                    v.tensor_tensor_reduce(lg[m % 2][:, 0:width[c]], unit_psum(m)[:, 0:width[c]],
                                           score[:, sbase[c]:sbase[c] + width[c]], 1.0, -3.4e38, ALU.add, ALU.max,
                                           small[:, mx + m % 2:mx + m % 2 + 1]).then_inc(c_max.sem, 1)
                    v.wait_ge(*c_max(L, m + 1))
                    v.tensor_scalar(small[:, nb + m % 2:nb + m % 2 + 1], small[:, mx + m % 2:mx + m % 2 + 1],
                                    -(HD ** -0.5), None, ALU.mult).then_inc(c_bias.sem, 1)

                def rows_out(c):
                    v.wait_ge(*c_pv(L, AH * (c + 1)))
                    if c >= 2:
                        v.wait_ge(*c_cat(L, c - 1))
                    v.reciprocal(small[:, rs:rs + AH], small[:, sm_ + AH * (c % 2):sm_ + AH * (c % 2) + AH]).then_inc(c_out.sem, 1)
                    v.wait_ge(*c_out(L, 2 * c + 1))
                    v.tensor_tensor(heads(oatt[c % 2], HD), heads(ps[:, 6 + c % 2, 0:256], HD),
                                    small[:, rs:rs + AH].rearrange("p (h e) -> p h e", e=1).broadcast_to([P, AH, HD]),
                                    ALU.mult).then_inc(c_out.sem, 1)

                def lo_rows(c):
                    v.wait_ge(*c_hi(L, c + 1))
                    v.tensor_tensor(act_lo[:, 2:4, c * P:(c + 1) * P], ps[:, 6 + c % 2, 256:512].rearrange("p (k n) -> p k n", n=P),
                                    act_hi[:, 2:4, c * P:(c + 1) * P].bitcast(F32), ALU.subtract).then_inc(c_lo.sem, 1)

                def attend(m):
                    c, h = divmod(m, AH)
                    maximum(m)
                    if h == 1 and c >= 1:
                        rows_out(c - 1)
                    if h == 2 and c >= 1:
                        lo_rows(c - 1)

                v.memset(max8[:, :], 0.0).then_inc(topk.sem, 1)
                v.wait_ge(*topk(L, 1))
                v.memset(small[:, 60:61], 0.0)
                for c in range(2, NT):
                    sc = score[:, sbase[c]:sbase[c] + width[c]]
                    rounds = TOPK // 8
                    pairs = range(ATT_BESIDE) if c == NT - 1 else ()

                    def top_round():
                        v.max(max8[:, :], sc)
                        v.drain()
                        v.match_replace(sc, max8[:, :], sc, TAKEN)
                        v.drain()

                    if not pairs:
                        with v.Fori(0, rounds // ROUNDS_AT_A_TIME) as r:
                            for _ in range(ROUNDS_AT_A_TIME):
                                top_round()
                    for i, m in enumerate(pairs):
                        for _ in range(rounds * i // len(pairs), rounds * (i + 1) // len(pairs)):
                            top_round()
                        attend(m)
                    v.tensor_scalar(sc, sc, TAKEN, NEG, ALU.not_equal, ALU.mult).then_inc(selected.sem, 1)
                for m in range(ATT_BESIDE, N_PAIRS):
                    attend(m)
                rows_out(NT - 1)
                lo_rows(NT - 1)

        chunk_in = [sig(f"chunk_in{s}", 16 * len(range(s, NT, PLACES))) for s in range(PLACES)]
        b_clear = sig("b_clear", PLACES + 2)
        chunk_done = sig("chunk_done", NT + 1)
        turned = sig("turned", 4 * NT)
        rowed = sig("rowed", 4 * NT)
        weighted = sig("weighted", 4 * NT)
        m_arg_ps = sig("m_arg_ps", NT)
        m_qk = sig("m_qk", NT)
        s_arg_ps = sig("s_arg_ps", NT)
        s_bc = sig("s_bc", NT)
        m_inter = sig("m_inter", NT)
        s_inter = sig("s_inter", NT)
        m_arg = sig("m_arg", NT)
        s_arg = sig("s_arg", NT)
        m_exp = sig("m_exp", NT)
        s_exp = sig("s_exp", NT)
        m_tri = sig("m_tri", NT)
        s_tri = sig("s_tri", NT)
        m_p = sig("m_p", NT)
        s_p = sig("s_p", NT)
        m_num = sig("m_num", NT)
        s_y = sig("s_y", NT)
        m_upd = sig("m_upd", NT)
        s_upd = sig("s_upd", NT)
        m_state = sig("m_state", 4 * NT)
        s_state = sig("s_state", 2 * NT)
        m_v = sig("m_v", 10 * NT)
        gated = sig("gated", NT)
        s_v = sig("s_v", 8 * NT)
        b_stat = sig("b_stat", 4 * NT)
        cat_ps = sig("cat_ps", 2 * NT)
        cat_hi = sig("cat_hi", 2 * NT)
        cat_lo = sig("cat_lo", NT)

        U_WO = N_PROJ
        wo_place = [raw[0], raw[1]] + wo_raw + [raw[0], raw[1]]
        wo_in = [sig(f"wo_in{k}", 16) for k in range(2, 6)]

        def wo_ready(k):
            if 2 <= k < 6:
                return wo_in[k - 2](L, 16)
            return raw_in[k % 2](L, raw_wait(U_WO + k % 2) + (16 if k >= 6 else 0))

        def load_w_out(sp, k):
            done = wo_in[k - 2] if 2 <= k < 6 else raw_in[k % 2]
            sp.dma_start(wo_place[k][:, :], row(L, w_out)[0, k * P:(k + 1) * P, :]).then_inc(done.sem, 16)

        bank = lambda i: ps[:, i, :]
        M_SS, M_RS, S_SS, S_RS = 32, 36, 40, 44
        DEN = 48

        with nc.Block() as block:
            @block.sync
            def _(sp):
                by_token = spill.rearrange("j p t -> p j t")
                load_w_out(sp, 0)
                load_w_out(sp, 1)
                for c in range(NT):
                    if c >= PLACES:
                        sp.wait_ge(*chunk_done(L, c - PLACES + 2))
                    sp.dma_start(wc[c % PLACES][:, :, :], by_token[:, :, c * P:(c + 1) * P]).then_inc(chunk_in[c % PLACES].sem, 16)

            def pipeline(engine, step, last):
                step(0, 0, 0)
                with engine.Fori(0, (NT - 2) // PLACES) as i:
                    for k in range(PLACES):
                        step(PLACES * i + k + 1, (k + 1) % PLACES, i + (k + 1) // PLACES)
                step(NT - 1, (NT - 1) % PLACES, (NT - 1) // PLACES)
                last()

            @block.gpsimd
            def _(pool):
                for s in range(PLACES):
                    pool.memset(vaug[s][:, :, HD:HD + 1], 1.0).then_inc(b_clear.sem, 1)
                pool.memset(cmem[:, :, :, :], 0.0).then_inc(b_clear.sem, 1)
                pool.memset(smem[:, :, :], 0.0).then_inc(b_clear.sem, 1)
                tri = cst[:, K_TRI:K_TRI + P].rearrange("p (o n) -> p o n", o=1)

                def step(c, s, n):
                    first = isinstance(c, int) and c == 0
                    if isinstance(c, int):
                        of = lambda t, q, n, w: t[:, c:c + 1, q, :].rearrange("p o (h e) -> p (o h) e", e=1)\
                            .broadcast_to([P, n, w])
                    else:
                        of = lambda t, q, n, w: t[:, bass.ds(c, 1), q, :].rearrange("p o (h e) -> p (o h) e", e=1)\
                            .broadcast_to([P, n, w])
                    pool.wait_ge(*rowed(L, 4 * c + 2))
                    if not first:
                        pool.wait_ge(*m_upd(L, c))
                    mk = rw[s][:, 6:8, :].rearrange("p a b -> p (a b)")
                    pool.tensor_tensor(wk[:, :, :], heads(mk, HD), of(gcol, 2, MH, HD), ALU.mult).then_inc(weighted.sem, 1)
                    xr = heads(rw[s][:, 0:4, :].rearrange("p a b -> p (a b)"), HD)
                    if not first:
                        pool.wait_ge(*s_y(L, c))
                    pool.tensor_tensor(xdt[:, :, :], xr, of(scol, 3, SH, HD), ALU.mult).then_inc(weighted.sem, 1)
                    pool.wait_ge(*m_exp(L, c + 1))
                    pool.tensor_tensor(pm[:, :, :], pm[:, :, :], tri.broadcast_to([P, MH, P]), ALU.mult).then_inc(m_tri.sem, 1)
                    pool.wait_ge(*s_exp(L, c + 1))
                    pool.tensor_tensor(pss[:, :, :], pss[:, :, :], tri.broadcast_to([P, SH, P]), ALU.mult).then_inc(s_tri.sem, 1)
                    if not first:
                        pool.wait_ge(*s_upd(L, c))
                    pool.tensor_tensor(xw[:, :, :], xr, of(scol, 2, SH, HD), ALU.mult).then_inc(weighted.sem, 1)
                    pool.wait_ge(*weighted(L, 4 * c + 3))
                    pool.tensor_tensor(xr, xr, dskip[:, :].rearrange("p (h e) -> p h e", e=1).broadcast_to([P, SH, HD]),
                                       ALU.mult).then_inc(weighted.sem, 1)

                pipeline(pool, step, lambda: None)

            @block.tensor
            def _(pe):
                pe.wait_ge(*b_clear(L, PLACES + 2))

                def turns(c, s, n):
                    w = wc[s]
                    pe.wait_ge(*chunk_in[s](L, 16 * n + 16))
                    if not (isinstance(c, int) and c == 0):
                        pe.wait_ge(*s_arg(L, c))
                        pe.wait_ge(*m_v(L, 10 * c - 9))
                        pe.wait_ge(*s_v(L, 8 * c - 7))
                    for b, js in enumerate(((0, 1, 2, 3), (4, 5, W_MK, W_MK + 1), (8, 9, 10, 11), (W_MV, W_MV + 1))):
                        for i, j in enumerate(js):
                            mm = pe.transpose(bank(b)[:, i * P:(i + 1) * P], w[:, j], ident)
                        mm.then_inc(turned.sem, 1)

                def begin(c, s):
                    w = wc[s]
                    first = isinstance(c, int) and c == 0
                    now = slice(c * P, (c + 1) * P) if isinstance(c, int) else bass.ds(c * P, P)
                    if not first:
                        pe.wait_ge(*m_v(L, 10 * c - 8))
                    for h in range(MH):
                        mm = pe.matmul(bank(5)[:, h * P:(h + 1) * P], cst[0:MH, K_SEL + P * h:K_SEL + P * (h + 1)],
                                       mrow[0:MH, now], start=True, stop=True)
                    mm.then_inc(m_arg_ps.sem, 1)
                    pe.wait_ge(*rowed(L, 4 * c + 2))
                    for h in range(SH):
                        mm = pe.matmul(bank(h // 4)[:, (h % 4) * P:(h % 4 + 1) * P],
                                       cst[0:SH, K_SEL + P * h:K_SEL + P * (h + 1)], arow[0:SH, now], start=True, stop=True)
                    mm.then_inc(s_arg_ps.sem, 1)
                    if not first:
                        pe.wait_ge(*s_state(L, 2 * c))
                        if not (isinstance(c, int) and c == 1):
                            pe.wait_ge(*chunk_done(L, c))
                    for h in range(MH):
                        q = slice(HD * (h % 2), HD * (h % 2) + HD)
                        mm = pe.matmul(bank(4 + 3 * (h % 2))[:, (h // 2) * P:(h // 2 + 1) * P], w[q, W_MK + h // 2], w[q, W_MQ + h // 2],
                                       start=True, stop=True)
                    mm.then_inc(m_qk.sem, 1)
                    if not first:
                        pe.wait_ge(*s_v(L, 8 * c - 6))
                    for g in range(SG):
                        mm = pe.matmul(bank(6)[:, g * P:(g + 1) * P], w[:, W_B + g], w[:, W_C + g], start=True, stop=True)
                    mm.then_inc(s_bc.sem, 1)

                def turn_m(c):
                    pe.wait_ge(*m_v(L, 10 * c + 10))
                    for i in range(2):
                        mm = pe.transpose(bank(6)[:, (2 + i) * P:(3 + i) * P], catr[:, i * P:(i + 1) * P], ident)
                    mm.then_inc(cat_ps.sem, 1)

                def turn_s(c):
                    pe.wait_ge(*s_v(L, 8 * c + 8))
                    for i in range(4):
                        mm = pe.transpose(bank(4)[:, i * P:(i + 1) * P], catr[:, (2 + i) * P:(3 + i) * P], ident)
                    mm.then_inc(cat_ps.sem, 1)

                def step(c, s, n):
                    w = wc[s]
                    first, last = (isinstance(c, int) and c == e for e in (0, NT - 1))
                    pe.wait_ge(*rowed(L, 4 * c + 4))
                    if not first:
                        pe.wait_ge(*m_state(L, 4 * c))
                    for p in range(2):
                        mm = pe.matmul(bank(2)[:, 130 * p:130 * (p + 1)], w[:, W_MQ + p],
                                       cmem[:, p].rearrange("p a b -> p (a b)"), start=True, stop=True)
                    mm.then_inc(m_inter.sem, 1)
                    if not first:
                        pe.wait_ge(*s_state(L, 2 * c))
                    for g in range(SG):
                        mm = pe.matmul(bank(3)[:, 256 * g:256 * (g + 1)], w[:, W_C + g],
                                       smem[:, 4 * g:4 * g + 4].rearrange("p a b -> p (a b)"), start=True, stop=True)
                    mm.then_inc(s_inter.sem, 1)
                    pe.wait_ge(*weighted(L, 4 * c + 1))
                    pe.wait_ge(*m_arg(L, c + 1))
                    for p in range(2):
                        mm = pe.matmul(bank(5)[:, 130 * p:130 * (p + 1)], wk[:, 2 * p:2 * p + 2].rearrange("p a b -> p (a b)"),
                                       vaug[s][:, 2 * p:2 * p + 2].rearrange("p a b -> p (a b)"), start=True, stop=True)
                    mm.then_inc(m_upd.sem, 1)
                    if not first:
                        turn_m(c - 1)
                    if not last:
                        turns(c + 1, (s + 1) % PLACES, n + (s + 1) // PLACES)
                    pe.wait_ge(*m_p(L, c + 1))
                    if not first:
                        turn_s(c - 1)
                    pe.wait_ge(*m_state(L, 4 * c + 4))
                    for h in range(MH):
                        mm = pe.matmul(bank(5)[:, 65 * h:65 * (h + 1)], pm[:, h], vaug[s][:, h], start=True, stop=True)
                    mm.then_inc(m_num.sem, 1)
                    pe.wait_ge(*weighted(L, 4 * c + 3))
                    for g in range(SG):
                        mm = pe.matmul(bank(7)[:, 256 * g:256 * (g + 1)], rw[s][:, 4 + g],
                                       xw[:, 4 * g:4 * g + 4].rearrange("p a b -> p (a b)"), start=True, stop=True)
                    mm.then_inc(s_upd.sem, 1)
                    pe.wait_ge(*s_p(L, c + 1))
                    for h in range(SH):
                        mm = pe.matmul(bank(6)[:, HD * h:HD * (h + 1)], pss[:, h], xdt[:, h], start=True, stop=True)
                    mm.then_inc(s_y.sem, 1)
                    if not last:
                        begin(c + 1, (s + 1) % PLACES)

                turns(0, 0, 0)
                begin(0, 0)
                def finish():
                    turn_m(NT - 1)
                    turn_s(NT - 1)

                pipeline(pe, step, finish)

            @block.scalar
            def _(act):
                act.preload_act_table_set("natural_log_exp_and_others")

                def rows(c, s):
                    for b, (dst, src) in enumerate((
                            (rw[s][:, 0:4], bank(0).rearrange("p (a b) -> p a b", b=P)),
                            (rw[s][:, 4:8], bank(1).rearrange("p (a b) -> p a b", b=P)),
                            (rw[s][:, 8:12], bank(2).rearrange("p (a b) -> p a b", b=P)),
                            (vaug[s][:, :, 0:HD], heads(bank(3)[:, 0:256], HD)))):
                        act.wait_ge(*turned(L, 4 * c + b + 1))
                        act.activation(dst, src, ACT.Copy).then_inc(rowed.sem, 1)

                def rsqrt(c, n, ss, rs, w, size):
                    act.activation(small[:, rs:rs + w], small[:, ss:ss + w], ACT.Ln, bias=EPS, scale=1.0 / size)\
                       .then_inc(b_stat.sem, 1)
                    act.wait_ge(*b_stat(L, 4 * c + n + 1))
                    act.activation(small[:, rs:rs + w], small[:, rs:rs + w], ACT.Exp, scale=-0.5).then_inc(b_stat.sem, 1)

                def hi(c):
                    now = slice(c * P, (c + 1) * P) if isinstance(c, int) else bass.ds(c * P, P)
                    act.wait_ge(*gated(L, c + 1))
                    act.activation(act_hi[:, 0:2, now], catf[:, :, :], ACT.Copy).then_inc(cat_hi.sem, 1)
                    act.wait_ge(*cat_ps(L, 2 * c + 2))
                    act.activation(act_hi[:, 4:8, now], tiles(bank(4)), ACT.Copy).then_inc(cat_hi.sem, 1)

                def step(c, s, n):
                    act.wait_ge(*m_arg(L, c + 1))
                    act.activation(pm[:, :, :], pm[:, :, :], ACT.Exp, scale=-1.0).then_inc(m_exp.sem, 1)
                    act.wait_ge(*s_arg(L, c + 1))
                    act.activation(pss[:, :, :], pss[:, :, :], ACT.Exp).then_inc(s_exp.sem, 1)
                    if not (isinstance(c, int) and c == 0):
                        hi(c - 1)
                    if not (isinstance(c, int) and c == NT - 1):
                        rows(c + 1, (s + 1) % PLACES)
                    act.wait_ge(*m_v(L, 10 * c + 8))
                    rsqrt(c, 0, M_SS, M_RS, MH, HD)
                    act.wait_ge(*s_v(L, 8 * c + 6))
                    rsqrt(c, 2, S_SS, S_RS, SG, 256)

                rows(0, 0)
                pipeline(act, step, lambda: hi(NT - 1))

            @block.vector
            def _(v):
                col = lambda k, n, w: small[:, k:k + n].rearrange("p (h e) -> p h e", e=1).broadcast_to([P, n, w])
                yf = y[:, :, :].rearrange("p a b -> p (a b)")

                def m_then(c, n, ins):
                    ins.then_inc(m_v.sem, 1)
                    v.wait_ge(*m_v(L, 10 * c + n))

                def s_then(c, n, ins):
                    ins.then_inc(s_v.sem, 1)
                    v.wait_ge(*s_v(L, 8 * c + n))

                def scale_out(c):
                    v.wait_ge(*b_stat(L, 4 * c + 2))
                    m_then(c, 9, v.tensor_tensor(heads(catr[:, 0:256], HD), heads(catr[:, 0:256], HD), col(M_RS, MH, HD), ALU.mult))
                    m_then(c, 10, v.tensor_tensor(catr[:, 0:256], catr[:, 0:256], mnw[:, :], ALU.mult))
                    v.wait_ge(*b_stat(L, 4 * c + 4))
                    s_then(c, 7, v.tensor_tensor(heads(yf, 256), heads(yf, 256), col(S_RS, SG, 256), ALU.mult))
                    s_then(c, 8, v.tensor_tensor(catr[:, 256:768], yf, snw[:, :], ALU.mult))

                def gate(c, s):
                    v.wait_ge(*cat_ps(L, 2 * c + 1))
                    v.tensor_tensor(catf[:, :, :], tiles(bank(6)[:, 256:512]), wc[s][:, W_MO:W_MO + 2], ALU.mult)\
                     .then_inc(gated.sem, 1)

                def lo(c):
                    now = slice(c * P, (c + 1) * P) if isinstance(c, int) else bass.ds(c * P, P)
                    v.wait_ge(*cat_hi(L, 2 * c + 1))
                    v.tensor_tensor(act_lo[:, 0:2, now], catf[:, :, :], act_hi[:, 0:2, now].bitcast(F32), ALU.subtract)\
                     .then_inc(cat_lo.sem, 1)
                    v.wait_ge(*cat_hi(L, 2 * c + 2))
                    v.tensor_tensor(act_lo[:, 4:8, now], tiles(bank(4)), act_hi[:, 4:8, now].bitcast(F32), ALU.subtract)\
                     .then_inc(chunk_done.sem, 1)

                def step(c, s, n):
                    at = slice(c, c + 1) if isinstance(c, int) else bass.ds(c, 1)
                    first = isinstance(c, int) and c == 0
                    one = lambda t, q, h: t[:, at, q, h:h + 1].rearrange("p o e -> p (o e)")
                    of = lambda t, q, n, w: t[:, at, q, :].rearrange("p o (h e) -> p (o h) e", e=1).broadcast_to([P, n, w])

                    v.wait_ge(*m_arg_ps(L, c + 1))
                    for h in range(MH):
                        ins = v.tensor_scalar(pm[:, h], bank(5)[:, h * P:(h + 1) * P], one(gcol, 0, h), 0.0,
                                              ALU.subtract, ALU.max)
                    ins.then_inc(m_arg.sem, 1)
                    v.wait_ge(*s_arg_ps(L, c + 1))
                    for h in range(SH):
                        ins = v.tensor_scalar(pss[:, h], bank(h // 4)[:, (h % 4) * P:(h % 4 + 1) * P], one(scol, 0, h),
                                              0.0, ALU.subtract, ALU.min)
                    ins.then_inc(s_arg.sem, 1)
                    if not first:
                        scale_out(c - 1)
                    v.wait_ge(*m_inter(L, c + 1))
                    m_then(c, 1, v.tensor_tensor(nd[:, :, :], heads(bank(2)[:, 0:260], 65), of(gcol, 1, MH, 65), ALU.mult))
                    v.wait_ge(*s_inter(L, c + 1))
                    s_then(c, 1, v.tensor_tensor(y[:, :, :], heads(bank(3), HD), of(scol, 1, SH, HD), ALU.mult))
                    v.wait_ge(*m_tri(L, c + 1))
                    v.wait_ge(*m_qk(L, c + 1))
                    for e in range(2):
                        ins = v.tensor_tensor(pm[:, e::2], pm[:, e::2], heads(bank(4 + 3 * e)[:, 0:256], P), ALU.mult)
                    ins.then_inc(m_p.sem, 1)
                    if not first:
                        gate(c - 1, (s - 1) % PLACES)
                    v.wait_ge(*m_upd(L, c + 1))
                    for p in range(2):
                        for e in range(2):
                            q = slice(HD * e, HD * e + HD)
                            v.scalar_tensor_tensor(
                                out=cmem[q, p, e], in0=cmem[q, p, e],
                                scalar=decm[q, p, at],
                                in1=bank(5)[q, 130 * p + 65 * e:130 * p + 65 * (e + 1)],
                                op0=ALU.mult, op1=ALU.add).then_inc(m_state.sem, 1)
                    v.wait_ge(*s_tri(L, c + 1))
                    v.wait_ge(*s_bc(L, c + 1))
                    for g in range(SG):
                        gt = bank(6)[:, g * P:(g + 1) * P].rearrange("p (o n) -> p o n", o=1).broadcast_to([P, 4, P])
                        ins = v.tensor_tensor(pss[:, 4 * g:4 * g + 4], pss[:, 4 * g:4 * g + 4], gt, ALU.mult)
                    ins.then_inc(s_p.sem, 1)
                    if not first:
                        lo(c - 1)
                    v.wait_ge(*m_num(L, c + 1))
                    m_then(c, 2, v.tensor_tensor(nd[:, :, :], nd[:, :, :], heads(bank(5)[:, 0:260], 65), ALU.add))
                    den = small[:, DEN:DEN + MH].rearrange("p (h e) -> p h e", e=1)
                    m_then(c, 3, v.scalar_tensor_tensor(out=den, in0=nd[:, :, HD:HD + 1], scalar=-1.0,
                                                        in1=nd[:, :, HD:HD + 1], op0=ALU.mult, op1=ALU.max))
                    m_then(c, 4, v.tensor_tensor(den, den, of(gcol, 3, MH, 1), ALU.max))
                    m_then(c, 5, v.reciprocal(small[:, DEN:DEN + MH], small[:, DEN:DEN + MH]))
                    m_then(c, 6, v.tensor_tensor(heads(catr[:, 0:256], HD), nd[:, :, 0:HD], col(DEN, MH, HD), ALU.mult))
                    hsq = nd[:, :, 0:HD]
                    m_then(c, 7, v.tensor_tensor(hsq, heads(catr[:, 0:256], HD), heads(catr[:, 0:256], HD), ALU.mult))
                    m_then(c, 8, v.tensor_reduce(small[:, M_SS:M_SS + MH], hsq, AX.X, ALU.add))
                    v.wait_ge(*s_upd(L, c + 1))
                    v.tensor_tensor(smem[:, :, :], smem[:, :, :],
                                    decs[:, :, at].broadcast_to([P, SH, HD]), ALU.mult).then_inc(s_state.sem, 1)
                    v.wait_ge(*s_state(L, 2 * c + 1))
                    v.tensor_tensor(smem[:, :, :], smem[:, :, :], heads(bank(7), HD), ALU.add).then_inc(s_state.sem, 1)
                    v.wait_ge(*s_y(L, c + 1))
                    s_then(c, 2, v.tensor_tensor(y[:, :, :], y[:, :, :], heads(bank(6), HD), ALU.add))
                    v.wait_ge(*weighted(L, 4 * c + 4))
                    s_then(c, 3, v.tensor_tensor(y[:, :, :], y[:, :, :], heads(rw[s][:, 0:4].rearrange("p a b -> p (a b)"), HD), ALU.add))
                    s_then(c, 4, v.tensor_tensor(y[:, :, :], y[:, :, :], heads(rw[s][:, 8:12].rearrange("p a b -> p (a b)"), HD), ALU.mult))
                    for g in range(SG):
                        yg = y[:, 4 * g:4 * g + 4].rearrange("p a b -> p (a b)")
                        v.tensor_tensor_reduce(catr[:, 256 * (1 + g):256 * (2 + g)], yg, yg, 1.0, 0.0,
                                               ALU.mult, ALU.add, small[:, S_SS + g:S_SS + g + 1]).then_inc(s_v.sem, 1)

                def finish():
                    scale_out(NT - 1)
                    gate(NT - 1, (NT - 1) % PLACES)
                    lo(NT - 1)

                v.memset(small[:, 60:61], 0.0).then_inc(chunk_done.sem, 1)
                pipeline(v, step, finish)

        U_FF = U_WO + KT
        assert U_FF % 2 == 0 and FB % 2 == 1
        wg_v = w_gate.rearrange("l (k p) f -> l p k f", p=P)
        wu_v = w_up.rearrange("l (k p) f -> l p k f", p=P)

        def ff_in(u, s):
            return 8 * u - 32 if s == 0 else 8 * (u + 1) - 16

        wo_lo_v = sig("wo_lo_v", KT)
        d_par = sig("d_par", 16 * 2)
        xr_in = [sig(f"xr_in{s}", 16 * NT // 2) for s in range(2)]
        x_out = [sig(f"x_out{s}", 16 * NT // 2) for s in range(2)]
        d_mm = sig("d_mm", NT)
        d_s1 = sig("d_s1", 3 * NT)
        d_mix = sig("d_mix", NT)
        d_x = sig("d_x", NT)
        d_s2 = sig("d_s2", 3 * NT)
        d_xn = sig("d_xn", NT)
        d_turn = sig("d_turn", NT)
        d_hi = sig("d_hi", NT)
        d_lo = sig("d_lo", NT)
        sp_end = sig("sp_end", 2)

        def turn_bank(t):
            return ps[:, 4 + 2 * (t % 2):6 + 2 * (t % 2), :].rearrange("p a b -> p (a b)")

        def stats(act, done, at_count, src, junk, s):
            act.activation(junk, src, ACT.Square, accum_out=small[:, s:s + 1]).then_inc(done.sem, 1)
            act.wait_ge(*done(L, at_count + 1))
            act.activation(small[:, s + 1:s + 2], small[:, s:s + 1], ACT.Ln, bias=EPS, scale=1.0 / D).then_inc(done.sem, 1)
            act.wait_ge(*done(L, at_count + 2))
            act.activation(small[:, s + 2:s + 3], small[:, s + 1:s + 2], ACT.Exp, scale=-0.5).then_inc(done.sem, 1)

        with nc.Block() as block:
            @block.sync
            def _(sp):
                def x_tile(t):
                    if t >= 2:
                        sp.wait_ge(*x_out[t % 2](L, 16 * (t // 2)))
                        sp.wait_ge(*d_xn(L, t - 1))
                    sp.dma_start(xres[t % 2][:, :], out[t * P:(t + 1) * P, :]).then_inc(xr_in[t % 2].sem, 16)

                for k in range(2, 6):
                    load_w_out(sp, k)
                for k in range(6, KT):
                    sp.wait_ge(*w_lo(L, U_WO + k - 5))
                    passed(sp)
                    sp.wait_ge(*wo_lo_v(L, k - 5))
                    passed(sp)
                    load_w_out(sp, k)
                sp.dma_start(nrow[0][:, :], row(L, norm_w)[:, 1].broadcast_to([P, D])).then_inc(d_par.sem, 16)
                sp.dma_start(nrow[1][:, :], row(L, norm_w)[:, 2].broadcast_to([P, D])).then_inc(d_par.sem, 16)
                x_tile(0)
                x_tile(1)
                for s, w in ((0, wg_v), (1, wu_v)):
                    sp.wait_ge(*w_lo(L, U_WO + 7 + s))
                    passed(sp)
                    sp.wait_ge(*wo_lo_v(L, 7 + s))
                    passed(sp)
                    sp.dma_start(tiles(raw[s][:, :]), row(L, w)[0, :, :, 0:P]).then_inc(raw_in[s].sem, 16)
                for t in range(NT):
                    sp.wait_ge(*d_x(L, t + 1))
                    sp.dma_start(xmid[t * P:(t + 1) * P, :], xres[t % 2][:, :]).then_inc(x_out[t % 2].sem, 16)
                    if t + 2 < NT:
                        x_tile(t + 2)
                for s in range(2):
                    sp.wait_ge(*x_out[s](L, 16 * NT // 2))
                    sp.sem_inc(sp_end.sem, 1)

            @block.gpsimd
            def _(pool):
                for k in range(KT):
                    u = U_WO + k
                    pool.wait_ge(*w_hi(L, u + 1))
                    pool.tensor_tensor(wolo[:, k, 0:HALF], wo_place[k][:, 0:HALF], wohi[:, k, 0:HALF].bitcast(F32),
                                       ALU.subtract).then_inc(w_lo.sem, 1)
                for s in range(2):
                    pool.wait_ge(*w_hi(L, U_FF + s + 1))
                    pool.tensor_tensor(wlo[s][:, :], raw[s][:, :], whi[s][:, :].bitcast(F32), ALU.subtract).then_inc(w_lo.sem, 1)

            @block.tensor
            def _(pe):
                def mix(t):
                    if t >= 2:
                        pe.wait_ge(*d_mix(L, t - 1))
                    rows = slice(t * P, (t + 1) * P)
                    for half in range(2):
                        cols = slice(half * HALF, (half + 1) * HALF)
                        for k in range(KT):
                            if t == 0 and half == 0:
                                pe.wait_ge(*w_lo(L, U_WO + k + 1))
                                pe.wait_ge(*wo_lo_v(L, k + 1))
                            for m, (a, w) in enumerate(((act_hi, wohi), (act_hi, wolo), (act_lo, wohi))):
                                mm = pe.matmul(ps[:, 2 * (t % 2) + half, :], a[:, k, rows], w[:, k, cols],
                                               start=(k == 0 and m == 0), stop=(k == KT - 1 and m == 2))
                    mm.then_inc(d_mm.sem, 1)

                def turn(t):
                    pe.wait_ge(*d_xn(L, t + 1))
                    if t >= 2:
                        pe.wait_ge(*d_lo(L, t - 1))
                    for j in range(KT):
                        mm = pe.transpose(tiles(turn_bank(t))[:, j], mixn[t % 2][:, j * P:(j + 1) * P], ident)
                    mm.then_inc(d_turn.sem, 1)

                mix(0)
                for t in range(NT):
                    if t + 1 < NT:
                        mix(t + 1)
                    turn(t)

            @block.scalar
            def _(act):
                act.preload_act_table_set("natural_log_exp_and_others")
                for k in range(KT):
                    act.wait_ge(*wo_ready(k))
                    act.activation(wohi[:, k], wo_place[k][:, :], ACT.Copy).then_inc(w_hi.sem, 1)
                for s in range(2):
                    act.wait_ge(*raw_in[s](L, ff_in(U_FF + s, s)))
                    act.activation(whi[s][:, :], raw[s][:, :], ACT.Copy).then_inc(w_hi.sem, 1)

                def hi(t):
                    act.wait_ge(*d_turn(L, t + 1))
                    act.activation(act_hi[:, :, t * P:(t + 1) * P], tiles(turn_bank(t)), ACT.Copy).then_inc(d_hi.sem, 1)

                for t in range(NT):
                    act.wait_ge(*d_mm(L, t + 1))
                    if t >= 2:
                        act.wait_ge(*d_turn(L, t - 1))
                    stats(act, d_s1, 3 * t, unit_psum(t), mixn[t % 2][:, :], 8 * (t % 2))
                    if t >= 1:
                        hi(t - 1)
                    act.wait_ge(*d_x(L, t + 1))
                    stats(act, d_s2, 3 * t, xres[t % 2][:, :], mixn[t % 2][:, :], 8 * (t % 2) + 4)
                hi(NT - 1)

            @block.vector
            def _(v):
                for k in range(KT):
                    v.wait_ge(*w_hi(L, U_WO + k + 1))
                    v.tensor_tensor(wolo[:, k, HALF:], wo_place[k][:, HALF:], wohi[:, k, HALF:].bitcast(F32),
                                    ALU.subtract).then_inc(wo_lo_v.sem, 1)
                v.wait_ge(*d_par(L, 32))

                def lo(t):
                    v.wait_ge(*d_hi(L, t + 1))
                    v.tensor_tensor(act_lo[:, :, t * P:(t + 1) * P], tiles(turn_bank(t)),
                                    act_hi[:, :, t * P:(t + 1) * P].bitcast(F32), ALU.subtract).then_inc(d_lo.sem, 1)

                for t in range(NT):
                    s = t % 2
                    v.wait_ge(*d_s1(L, 3 * t + 3))
                    v.scalar_tensor_tensor(out=mixn[s][:, :], in0=unit_psum(t), scalar=small[:, 8 * s + 2:8 * s + 3],
                                           in1=nrow[0][:, :], op0=ALU.mult, op1=ALU.mult).then_inc(d_mix.sem, 1)
                    v.wait_ge(*d_mix(L, t + 1))
                    v.wait_ge(*xr_in[s](L, 16 * (t // 2 + 1)))
                    v.tensor_tensor(xres[s][:, :], xres[s][:, :], mixn[s][:, :], ALU.add).then_inc(d_x.sem, 1)
                    if t >= 1:
                        lo(t - 1)
                    v.wait_ge(*d_s2(L, 3 * t + 3))
                    v.scalar_tensor_tensor(out=mixn[s][:, :], in0=xres[s][:, :], scalar=small[:, 8 * s + 6:8 * s + 7],
                                           in1=nrow[1][:, :], op0=ALU.mult, op1=ALU.mult).then_inc(d_xn.sem, 1)
                lo(NT - 1)

        e_par = sig("e_par", 16)
        silu = sig("silu", 2 * FB)
        hidden = sig("hidden", 2 * FB)
        h_hi = sig("h_hi", 2 * FB)
        h_lo = sig("h_lo", 2 * FB)
        y_ps = sig("y_ps", NT * FB)
        y_add = sig("y_add", 2 + NT * FB)
        e_stat = sig("e_stat", 3 * NT)
        e_yn = sig("e_yn", NT)
        e_x = sig("e_x", NT)
        e_in = [sig(f"e_in{s}", 16 * NT // 2) for s in range(2)]
        e_out = [sig(f"e_out{s}", 16 * NT // 2) for s in range(2)]
        e_end = sig("e_end", 2)
        resid = [a[:, :] for a in own + [hf] + raw]

        with nc.Block() as block:
            @block.sync
            def _(sp):
                def load(u, s, src, tiled):
                    sp.wait_ge(*w_lo(L, u - 1))
                    passed(sp)
                    dst = tiles(raw[s][:, :]) if tiled else raw[s][:, :]
                    sp.dma_start(dst, src).then_inc(raw_in[s].sem, 16)

                def gate_up(b, u):
                    for j in range(1 if isinstance(b, int) else 0, 2):
                        cols = bass.ds(256 * b + P * j, P)
                        load(u + 2 * j, 0, row(L, wg_v)[0, :, :, cols], True)
                        load(u + 2 * j + 1, 1, row(L, wu_v)[0, :, :, cols], True)

                def down(b, u):
                    for j in range(2):
                        load(u + j, j, row(L, w_down)[0, bass.ds(256 * b + P * j, P), :], False)

                gate_up(0, U_FF)
                sp.dma_start(nrow[0][:, :], row(L, norm_w)[:, 3].broadcast_to([P, D])).then_inc(e_par.sem, 16)
                with sp.Fori(1, FB) as b:
                    u = U_FF + 6 * b - 2
                    gate_up(b, u)
                    down(b - 1, u + 4)
                down(FB - 1, N_UNITS - 2)
                for t in range(NT):
                    if t == NT - 3:
                        sp.wait_ge(*h_lo(L, 2 * FB))
                    if t == NT - 2:
                        sp.wait_ge(*w_lo(L, N_UNITS))
                    sp.dma_start(resid[t], xmid[t * P:(t + 1) * P, :]).then_inc(e_in[t % 2].sem, 16)
                for t in range(NT):
                    sp.wait_ge(*e_x(L, t + 1))
                    sp.dma_start(out[t * P:(t + 1) * P, :], resid[t]).then_inc(e_out[t % 2].sem, 16)
                for s in range(2):
                    sp.wait_ge(*e_out[s](L, 16 * NT // 2))
                    sp.sem_inc(e_end.sem, 1)

            @block.gpsimd
            def _(pool):
                def ring_lo(u, s, lo_t, hi_t):
                    pool.wait_ge(*w_hi(L, u + 1))
                    pool.tensor_tensor(lo_t[s][:, :], raw[s][:, :], hi_t[s][:, :].bitcast(F32), ALU.subtract)\
                        .then_inc(w_lo.sem, 1)

                def hid_lo(b, j, p):
                    pool.wait_ge(*h_hi(L, 2 * b + j + 1))
                    pool.tensor_tensor(hlo[p][:, j], hf[:, :], hhi[p][:, j].bitcast(F32), ALU.subtract).then_inc(h_lo.sem, 1)

                def body(b, p, u):
                    if not isinstance(b, int):
                        ring_lo(u, 0, wlo, whi)
                        ring_lo(u + 1, 1, wlo, whi)
                    ring_lo(u + 2, 0, wlo, whi)
                    hid_lo(b, 0, p)
                    ring_lo(u + 3, 1, wlo, whi)
                    if not (isinstance(b, int) and b == 0):
                        ring_lo(u + 4, 0, dlo, dhi)
                        ring_lo(u + 5, 1, dlo, dhi)
                    hid_lo(b, 1, p)

                for i in range(2):
                    pool.memset(yacc[:, 4 * i:4 * i + 4], 0.0).then_inc(y_add.sem, 1)
                body(0, 0, U_FF)
                with pool.Fori(0, FB // 2) as i:
                    for p in range(2):
                        b = 2 * i + p + 1
                        body(b, (p + 1) % 2, U_FF + 6 * b - 2)
                for j in range(2):
                    ring_lo(N_UNITS - 2 + j, j, dlo, dhi)
                for t in range(NT):
                    pool.wait_ge(*e_yn(L, t + 1))
                    pool.wait_ge(*e_in[t % 2](L, 16 * (NT // 2)))
                    pool.tensor_tensor(resid[t], resid[t], yacc[:, t], ALU.add).then_inc(e_x.sem, 1)

            @block.scalar
            def _(act):
                def ring_hi(u, s, hi_t):
                    act.wait_ge(*raw_in[s](L, ff_in(u, s)))
                    act.activation(hi_t[s][:, :], raw[s][:, :], ACT.Copy).then_inc(w_hi.sem, 1)

                def gate(b, j):
                    act.wait_ge(*pj(L, N_PROJ + 4 * b + 2 * j + 1))
                    if not (isinstance(b, int) and b == 0 and j == 0):
                        act.wait_ge(*hidden(L, 2 * b + j))
                    act.activation(sg[:, :], unit_psum(0), ACT.Silu).then_inc(silu.sem, 1)

                def hid_hi(b, j, p):
                    act.wait_ge(*hidden(L, 2 * b + j + 1))
                    act.activation(hhi[p][:, j], hf[:, :], ACT.Copy).then_inc(h_hi.sem, 1)

                def body(b, p, u):
                    first = isinstance(b, int) and b == 0
                    if not first:
                        act.wait_ge(*pj(L, N_PROJ + 4 * b - 1))
                        ring_hi(u, 0, whi)
                        act.wait_ge(*pj(L, N_PROJ + 4 * b))
                        ring_hi(u + 1, 1, whi)
                    gate(b, 0)
                    ring_hi(u + 2, 0, whi)
                    hid_hi(b, 0, p)
                    act.wait_ge(*pj(L, N_PROJ + 4 * b + 2))
                    ring_hi(u + 3, 1, whi)
                    gate(b, 1)
                    if not first:
                        ring_hi(u + 4, 0, dhi)
                        ring_hi(u + 5, 1, dhi)
                    hid_hi(b, 1, p)

                body(0, 0, U_FF)
                with act.Fori(0, FB // 2) as i:
                    for p in range(2):
                        b = 2 * i + p + 1
                        body(b, (p + 1) % 2, U_FF + 6 * b - 2)
                act.wait_ge(*y_ps(L, NT * (FB - 1)))
                for j in range(2):
                    ring_hi(N_UNITS - 2 + j, j, dhi)
                act.preload_act_table_set("natural_log_exp_and_others")
                for t in range(NT):
                    act.wait_ge(*y_add(L, 2 + NT * (FB - 1) + t + 1))
                    stats(act, e_stat, 3 * t, yacc[:, t], sg[:, :], 4 * t)

            @block.tensor
            def _(pe):
                def gate_up(b, u):
                    for j in range(2):
                        for s in range(2):
                            pe.wait_ge(*w_lo(L, u + 2 * j + s + 1))
                            if not (isinstance(b, int) and b == 0 and j == 0):
                                pe.wait_ge(*(silu if s == 0 else hidden)(L, 2 * b + j))
                            wh, wl = tiles(whi[s][:, :]), tiles(wlo[s][:, :])
                            for half in range(2):
                                cols = slice(half * HALF, (half + 1) * HALF)
                                for k in range(KT):
                                    for m, (w, a) in enumerate(((wh, act_hi), (wh, act_lo), (wl, act_hi))):
                                        mm = pe.matmul(ps[:, 2 * s + half, :], w[:, k], a[:, k, cols],
                                                       start=(k == 0 and m == 0), stop=(k == KT - 1 and m == 2))
                            mm.then_inc(pj.sem, 1)

                def down(b, p, u):
                    pe.wait_ge(*w_lo(L, u + 2))
                    pe.wait_ge(*h_lo(L, 2 * b + 2))
                    for t in range(NT):
                        pe.wait_ge(*y_add(L, NT * b + t + 1))
                        rows = slice(t * P, (t + 1) * P)
                        for half in range(2):
                            cols = slice(half * HALF, (half + 1) * HALF)
                            for j in range(2):
                                for m, (h, w) in enumerate(((hhi, dhi), (hhi, dlo), (hlo, dhi))):
                                    mm = pe.matmul(ps[:, 4 + 2 * (t % 2) + half, :], h[p][:, j, rows], w[j][:, cols],
                                                   start=(j == 0 and m == 0), stop=(j == 1 and m == 2))
                        mm.then_inc(y_ps.sem, 1)

                gate_up(0, U_FF)
                with pe.Fori(0, FB // 2) as i:
                    for p in range(2):
                        b = 2 * i + p + 1
                        u = U_FF + 6 * b - 2
                        gate_up(b, u)
                        down(b - 1, p, u + 4)
                down(FB - 1, 0, N_UNITS - 2)

            @block.vector
            def _(v):
                def hid(b, j):
                    v.wait_ge(*silu(L, 2 * b + j + 1))
                    v.wait_ge(*pj(L, N_PROJ + 4 * b + 2 * j + 2))
                    if not (isinstance(b, int) and b == 0 and j == 0):
                        v.wait_ge(*h_lo(L, 2 * b + j))
                    v.tensor_tensor(hf[:, :], sg[:, :], unit_psum(1), ALU.mult).then_inc(hidden.sem, 1)

                def add_tile(b, t):
                    v.wait_ge(*y_ps(L, NT * b + t + 1))
                    if t == 0:
                        v.wait_ge(*y_add(L, NT * b + 2))
                    v.tensor_tensor(yacc[:, t], yacc[:, t], turn_bank(t), ALU.add).then_inc(y_add.sem, 1)

                def add(b):
                    for t in range(NT):
                        add_tile(b, t)

                hid(0, 0)
                hid(0, 1)
                with v.Fori(1, FB) as b:
                    hid(b, 0)
                    hid(b, 1)
                    add(b - 1)
                v.wait_ge(*e_par(L, 16))
                for t in range(NT + 1):
                    if t < NT:
                        add_tile(FB - 1, t)
                    if t >= 1:
                        v.wait_ge(*e_stat(L, 3 * t))
                        v.scalar_tensor_tensor(out=yacc[:, t - 1], in0=yacc[:, t - 1], scalar=small[:, 4 * t - 2:4 * t - 1],
                                               in1=nrow[0][:, :], op0=ALU.mult, op1=ALU.mult).then_inc(e_yn.sem, 1)


_INS = ["x", "positions", "norm_w", "w_in", "mlstm_gate_bias", "mlstm_norm_w", "conv_w", "conv_b", "dt_bias", "a_log",
        "d_skip", "ssd_norm_w", "w_out", "w_gate", "w_up", "w_down"]


def kernel(**inputs):
    import concourse.bacc as _bacc
    from concourse.bass_utils import run_bass_kernel_spmd as _run

    nc = _bacc.Bacc("TRN2", target_bir_lowering=False, num_devices=1, dynamic_dma_scratch_size=1024)
    arrays, args = {}, []
    host = {name: np.ascontiguousarray(inputs[name]) for name in _INS}
    host["x"] = host["x"].reshape(S, D)
    host["table"] = constant_table()
    for name, a in host.items():
        arrays[f"in_{name}"] = a
        args.append(nc.dram_tensor(f"in_{name}", a.shape, mybir.dt.from_np(a.dtype), kind="ExternalInput").ap())
    out = nc.dram_tensor("out", (S, D), F32, kind="ExternalOutput").ap()
    build(nc, *args, out)
    r = _run(nc, [arrays], core_ids=[0])
    return r.results[0]["out"].reshape(1, S, D)
```
